# Optimizing a Trainium2 kernel written in Bass

```python
import math
import jax, jax.numpy as jnp
from jax import lax
import numpy as np
import jax
import jax.numpy as jnp

D_MODEL = 1024
BATCH = 1
SEQ = 256
DEPTH = 2

HEAD_DIM = 64
N_HEADS_TOTAL = D_MODEL // HEAD_DIM
N_SB_HEADS = N_HEADS_TOTAL // 4
DIL_GROUPS = ((128, 1), (512, 4), (2048, 16))
N_DIL_GROUPS = len(DIL_GROUPS)
HEADS_PER_GROUP = (N_HEADS_TOTAL - N_SB_HEADS) // N_DIL_GROUPS
N_DIL_HEADS = HEADS_PER_GROUP * N_DIL_GROUPS
D_DIL = N_DIL_HEADS * HEAD_DIM
D_DIL_OUT = HEADS_PER_GROUP * HEAD_DIM
D_SB = N_SB_HEADS * HEAD_DIM
D_IN = 3 * D_DIL + 3 * D_SB + 2 * D_MODEL
D_FF = 128 * ((8 * D_MODEL // 3 + 127) // 128)
ROPE_THETA = 500000.0
ROPE_DIM = HEAD_DIM // 4
Q_BLOCK = 128
RMS_EPS = 1e-6


def rms_norm(x, gain):
    xf = x.astype(jnp.float32)
    xf = xf * lax.rsqrt(jnp.mean(xf * xf, axis=-1, keepdims=True) + RMS_EPS)
    return (xf * gain.astype(jnp.float32)).astype(x.dtype)

def swiglu(x, w_gate, w_up, w_down):
    return (jax.nn.silu(x @ w_gate) * (x @ w_up)) @ w_down

def rope_tables(seq_len):
    pos = jnp.arange(seq_len, dtype=jnp.float32)
    inv_freq = ROPE_THETA ** (-jnp.arange(0, ROPE_DIM, 2, dtype=jnp.float32) / ROPE_DIM)
    ang = pos[:, None] * inv_freq[None, :]
    return jnp.cos(ang), jnp.sin(ang)

def apply_partial_rope(x, cos, sin):
    half = ROPE_DIM // 2
    x1 = x[..., :half]
    x2 = x[..., half:ROPE_DIM]
    c = cos.astype(x.dtype)
    s = sin.astype(x.dtype)
    return jnp.concatenate([x1 * c - x2 * s, x2 * c + x1 * s, x[..., ROPE_DIM:]], axis=-1)

def dilated_window_attention(q, k, v, window, dilation):
    B, H, T, dh = q.shape
    span = window // dilation
    unit = span * dilation
    t_pad = -(-T // unit) * unit
    n_sub = t_pad // dilation
    n_blk = n_sub // span

    def to_blocks(a):
        a = jnp.pad(a, ((0, 0), (0, 0), (0, t_pad - T), (0, 0)))
        a = a.reshape(B, H, n_sub, dilation, dh).transpose(0, 1, 3, 2, 4)
        return a.reshape(B, H, dilation, n_blk, span, dh)

    qb, kb, vb = to_blocks(q), to_blocks(k), to_blocks(v)

    def with_prev(a):
        prev = jnp.pad(a, ((0, 0), (0, 0), (0, 0), (1, 0), (0, 0), (0, 0)))[:, :, :, :-1]
        return jnp.concatenate([prev, a], axis=4)

    kw, vw = with_prev(kb), with_prev(vb)
    s = jnp.einsum('bhrnqd,bhrnkd->bhrnqk', qb, kw).astype(jnp.float32) * (dh ** -0.5)
    qi = jnp.arange(span)[:, None]
    kj = jnp.arange(2 * span)[None, :]
    dist = qi + span - kj
    band = (dist >= 0) & (dist <= span)
    blk = jnp.arange(n_blk)[:, None, None]
    valid = band[None] & ((blk > 0) | (kj >= span)[None])
    s = jnp.where(valid, s, -jnp.inf)
    m = jnp.max(s, axis=-1, keepdims=True)
    p = jnp.exp(s - m)
    denom = jnp.sum(p, axis=-1, keepdims=True)
    o = jnp.einsum('bhrnqk,bhrnkd->bhrnqd', p, vw.astype(jnp.float32)) / denom
    lse = (m + jnp.log(denom))[..., 0]
    o = o.reshape(B, H, dilation, n_sub, dh).transpose(0, 1, 3, 2, 4).reshape(B, H, t_pad, dh)[:, :, :T]
    lse = lse.reshape(B, H, dilation, n_sub).transpose(0, 1, 3, 2).reshape(B, H, t_pad)[:, :, :T]
    return o, lse

def stick_breaking_attention(q, k, v):
    B, H, T, dh = q.shape
    n_blk = T // Q_BLOCK
    qb = q.reshape(B, H, n_blk, Q_BLOCK, dh).transpose(2, 0, 1, 3, 4)
    kpos = jnp.arange(T)
    vf = v.astype(jnp.float32)

    def block(args):
        q_blk, b = args
        z = jnp.einsum('bhqd,bhkd->bhqk', q_blk, k).astype(jnp.float32) * (dh ** -0.5)
        qpos = b * Q_BLOCK + jnp.arange(Q_BLOCK)
        past = kpos[None, :] < qpos[:, None]
        log_beta = jax.nn.log_sigmoid(z)
        log_keep = jnp.where(past, jax.nn.log_sigmoid(-z), 0.0)
        after = lax.cumsum(log_keep, axis=3, reverse=True) - log_keep
        w = jnp.where(past, jnp.exp(log_beta + after), 0.0)
        return jnp.einsum('bhqk,bhkd->bhqd', w, vf)

    o = lax.map(block, (qb, jnp.arange(n_blk)))
    return o.transpose(1, 2, 0, 3, 4).reshape(B, H, T, dh).astype(q.dtype)

def hybrid_mixer(h, w_in, w_proj_dil, w_proj_sb, w_out, cos, sin):
    B, T, _ = h.shape
    proj = h @ w_in
    o1 = 3 * D_DIL
    o2 = o1 + 3 * D_SB
    o3 = o2 + D_MODEL
    qkv_d = proj[..., :o1].reshape(B, T, 3, N_DIL_HEADS, HEAD_DIM).transpose(2, 0, 3, 1, 4)
    q_d = apply_partial_rope(qkv_d[0], cos, sin)
    k_d = apply_partial_rope(qkv_d[1], cos, sin)
    v_d = qkv_d[2]
    outs, lses = [], []
    for g, (window, dilation) in enumerate(DIL_GROUPS):
        hs = slice(g * HEADS_PER_GROUP, (g + 1) * HEADS_PER_GROUP)
        o, lse = dilated_window_attention(q_d[:, hs], k_d[:, hs], v_d[:, hs], window, dilation)
        outs.append(o)
        lses.append(lse)
    w_grp = jax.nn.softmax(jnp.stack(lses, axis=0), axis=0)
    o_dil = jnp.sum(w_grp[..., None] * jnp.stack(outs, axis=0), axis=0).astype(h.dtype)
    o_dil = o_dil.transpose(0, 2, 1, 3).reshape(B, T, D_DIL_OUT)
    qkv_s = proj[..., o1:o2].reshape(B, T, 3, N_SB_HEADS, HEAD_DIM).transpose(2, 0, 3, 1, 4)
    o_sb = stick_breaking_attention(qkv_s[0], qkv_s[1], qkv_s[2])
    o_sb = o_sb.transpose(0, 2, 1, 3).reshape(B, T, D_SB)
    gate_dil = jax.nn.sigmoid(proj[..., o2:o3])
    gate_sb = jax.nn.sigmoid(proj[..., o3:])
    y = gate_dil * (o_dil @ w_proj_dil) + gate_sb * (o_sb @ w_proj_sb)
    return y @ w_out

def first_inputs(seed: int = 0) -> dict:
    key = jax.random.key(seed)
    ks = jax.random.split(key, 16)
    f32 = jnp.float32

    def dense(k, shape, fan_in):
        return jax.random.normal(k, shape, f32) * (fan_in ** -0.5)

    def gain(k, shape):
        return 1.0 + 0.05 * jax.random.normal(k, shape, f32)

    return {
        "x": jax.random.normal(ks[0], (BATCH, SEQ, D_MODEL), f32),
        "norm_ffn1": gain(ks[1], (DEPTH, D_MODEL)),
        "ffn1_w_gate": dense(ks[2], (DEPTH, D_MODEL, D_FF), D_MODEL),
        "ffn1_w_up": dense(ks[3], (DEPTH, D_MODEL, D_FF), D_MODEL),
        "ffn1_w_down": dense(ks[4], (DEPTH, D_FF, D_MODEL), D_FF),
        "norm_mix": gain(ks[5], (DEPTH, D_MODEL)),
        "w_in": dense(ks[6], (DEPTH, D_MODEL, D_IN), D_MODEL),
        "w_proj_dil": dense(ks[7], (DEPTH, D_DIL_OUT, D_MODEL), D_DIL_OUT),
        "w_proj_sb": dense(ks[8], (DEPTH, D_SB, D_MODEL), D_SB),
        "w_out": dense(ks[9], (DEPTH, D_MODEL, D_MODEL), D_MODEL),
        "norm_ffn2": gain(ks[10], (DEPTH, D_MODEL)),
        "ffn2_w_gate": dense(ks[11], (DEPTH, D_MODEL, D_FF), D_MODEL),
        "ffn2_w_up": dense(ks[12], (DEPTH, D_MODEL, D_FF), D_MODEL),
        "ffn2_w_down": dense(ks[13], (DEPTH, D_FF, D_MODEL), D_FF),
        "norm_final": gain(ks[14], (D_MODEL,)),
    }

def first_block(x, norm_ffn1, ffn1_w_gate, ffn1_w_up, ffn1_w_down, norm_mix, w_in,
              w_proj_dil, w_proj_sb, w_out, norm_ffn2, ffn2_w_gate, ffn2_w_up,
              ffn2_w_down, norm_final):
    T = x.shape[1]
    cos, sin = rope_tables(T)
    for l in range(DEPTH):
        x = x + 0.5 * swiglu(rms_norm(x, norm_ffn1[l]), ffn1_w_gate[l], ffn1_w_up[l], ffn1_w_down[l])
        x = x + hybrid_mixer(rms_norm(x, norm_mix[l]), w_in[l], w_proj_dil[l], w_proj_sb[l],
                             w_out[l], cos, sin)
        x = x + 0.5 * swiglu(rms_norm(x, norm_ffn2[l]), ffn2_w_gate[l], ffn2_w_up[l], ffn2_w_down[l])
    return rms_norm(x, norm_final)


ROPE_THETA_2 = 10000.0
NORM_EPS = 1e-6
NEG = -1e30
BRANCH_W = D_MODEL // 2
N_BRANCH = 4
NSA_HEADS = BRANCH_W // HEAD_DIM
NSA_KV = 2
NSA_R = NSA_HEADS // NSA_KV
CMP_LEN = 32
CMP_STRIDE = 16
CMP_HIDDEN = 256
SEL_LEN = 64
SEL_TOPK = 16
NSA_WINDOW = 512
SEL_Q_CHUNK = 32
FORCE_BONUS = 1e3
SWA_HEADS = BRANCH_W // HEAD_DIM
SWA_KV = 2
SWA_R = SWA_HEADS // SWA_KV
SWA_WINDOW = 128
CONV_CH = BRANCH_W
CONV_WIDTH = 31
POOL_CH = BRANCH_W
POOL_WINDOWS = (2, 4, 8, 16)
POOL_GROUPS = 4
POOL_GROUP_CH = POOL_CH // POOL_GROUPS
D_FF_2 = ((8 * D_MODEL // 3) + 127) // 128 * 128
FFN_CONV_WIDTH = 3
IN_SIZES = (
    NSA_HEADS * HEAD_DIM,
    3 * 2 * NSA_KV * HEAD_DIM,
    3 * NSA_HEADS,
    SWA_HEADS * HEAD_DIM,
    2 * SWA_KV * HEAD_DIM,
    2 * CONV_CH,
    POOL_CH,
)
IN_COLS = sum(IN_SIZES)


def rms_norm_2(x, g):
    xf = x.astype(jnp.float32)
    y = xf * lax.rsqrt(jnp.mean(xf * xf, axis=-1, keepdims=True) + NORM_EPS)
    return (y * g.astype(jnp.float32)).astype(x.dtype)

def layer_norm(x, g, b):
    xf = x.astype(jnp.float32)
    mu = jnp.mean(xf, axis=-1, keepdims=True)
    var = jnp.mean(jnp.square(xf - mu), axis=-1, keepdims=True)
    y = (xf - mu) * lax.rsqrt(var + NORM_EPS)
    return (y * g.astype(jnp.float32) + b.astype(jnp.float32)).astype(x.dtype)

def rope_tables_2(seq):
    inv = 1.0 / (ROPE_THETA_2 ** (jnp.arange(0, HEAD_DIM, 2, dtype=jnp.float32) / HEAD_DIM))
    ang = jnp.arange(seq, dtype=jnp.float32)[:, None] * inv[None, :]
    return jnp.cos(ang), jnp.sin(ang)

def apply_rope(x, cos, sin):
    shp = (1, x.shape[1]) + (1,) * (x.ndim - 3) + (HEAD_DIM // 2,)
    c, s = cos.reshape(shp), sin.reshape(shp)
    xf = x.astype(jnp.float32)
    x1, x2 = xf[..., : HEAD_DIM // 2], xf[..., HEAD_DIM // 2:]
    return jnp.concatenate([x1 * c - x2 * s, x2 * c + x1 * s], axis=-1).astype(x.dtype)

def causal_depthwise_conv(x, w, b):
    k, c = w.shape
    y = lax.conv_general_dilated(
        x, w[:, None, :].astype(x.dtype), window_strides=(1,), padding=[(k - 1, 0)],
        dimension_numbers=("NWC", "WIO", "NWC"), feature_group_count=c)
    return y + b.astype(x.dtype)

def masked_softmax(s, mask):
    p = jax.nn.softmax(jnp.where(mask, s, NEG), axis=-1)
    return jnp.where(mask, p, 0.0)

def banded_attention(q, k, v, window, sinks):
    bsz, seq, g, r, dk = q.shape
    span = window + Q_BLOCK
    k_pad = jnp.pad(k, ((0, 0), (window, 0), (0, 0), (0, 0)))
    v_pad = jnp.pad(v, ((0, 0), (window, 0), (0, 0), (0, 0)))
    scale = dk ** -0.5

    def block(i):
        start = i * Q_BLOCK
        qb = lax.dynamic_slice_in_dim(q, start, Q_BLOCK, axis=1)
        kb = lax.dynamic_slice_in_dim(k_pad, start, span, axis=1)
        vb = lax.dynamic_slice_in_dim(v_pad, start, span, axis=1)
        t = start + jnp.arange(Q_BLOCK)
        j = start - window + jnp.arange(span)
        mask = (j[None, :] <= t[:, None]) & (j[None, :] > t[:, None] - window) & (j[None, :] >= 0)
        mask = mask[None, None, None]
        s = jnp.einsum("bqgrd,bkgd->bgrqk", qb, kb, preferred_element_type=jnp.float32) * scale
        if sinks is None:
            p = masked_softmax(s, mask)
        else:
            sink = sinks.astype(jnp.float32).reshape(g, r)[None, :, :, None, None]
            s = jnp.where(mask, s, NEG)
            m = jnp.maximum(jnp.max(s, axis=-1, keepdims=True), sink)
            e = jnp.exp(s - m)
            p = e / (jnp.sum(e, axis=-1, keepdims=True) + jnp.exp(sink - m))
        return jnp.einsum("bgrqk,bkgd->bqgrd", p.astype(v.dtype), vb)

    out = lax.map(block, jnp.arange(seq // Q_BLOCK))
    return jnp.moveaxis(out, 0, 1).reshape(bsz, seq, g, r, dk)

def nsa_compress(k, pos, w1, w2):
    bsz, seq, g, dk = k.shape
    n_cmp = (seq - CMP_LEN) // CMP_STRIDE + 1
    idx = np.arange(n_cmp)[:, None] * CMP_STRIDE + np.arange(CMP_LEN)[None, :]
    blk = jnp.swapaxes(k[:, idx], 2, 3) + pos.astype(k.dtype)
    flat = blk.reshape(bsz, n_cmp, g, CMP_LEN * dk)
    return jax.nn.gelu(flat @ w1, approximate=True) @ w2

def nsa_compressed_attention(q, kc, vc):
    seq, n_cmp = q.shape[1], kc.shape[1]
    t = jnp.arange(seq)
    blk_end = jnp.arange(n_cmp) * CMP_STRIDE + CMP_LEN - 1
    mask = (blk_end[None, :] <= t[:, None])[None, :, None, None, :]
    s = jnp.einsum("bsgrd,bngd->bsgrn", q, kc, preferred_element_type=jnp.float32) * HEAD_DIM ** -0.5
    p = masked_softmax(s, mask)
    o = jnp.einsum("bsgrn,bngd->bsgrd", p.astype(vc.dtype), vc)
    return o, p

def nsa_select_blocks(p_cmp, seq):
    n_cmp = p_cmp.shape[-1]
    n_slc = seq // SEL_LEN
    i = jnp.arange(n_cmp)
    j = jnp.arange(n_slc)
    overlap = ((i[:, None] * CMP_STRIDE < (j[None, :] + 1) * SEL_LEN)
               & (i[:, None] * CMP_STRIDE + CMP_LEN > j[None, :] * SEL_LEN)).astype(jnp.float32)
    imp = jnp.einsum("bsgrn,nj->bsgj", p_cmp, overlap)
    cur = jnp.arange(seq) // SEL_LEN
    valid = (j[None, :] <= cur[:, None])[None, :, None, :]
    forced = ((j[None, :] == 0) | (j[None, :] == cur[:, None]) | (j[None, :] == cur[:, None] - 1))[None, :, None, :]
    score = jnp.where(valid, imp + jnp.where(forced, FORCE_BONUS, 0.0), -1.0)
    _, sel = lax.top_k(score, min(SEL_TOPK, n_slc))
    return sel

def nsa_selected_attention(q, k, v, sel):
    bsz, seq, g, r, dk = q.shape
    n_slc = seq // SEL_LEN
    n_top = sel.shape[-1]
    kb = k.reshape(bsz, n_slc, SEL_LEN, g, dk).transpose(0, 3, 1, 2, 4)
    vb = v.reshape(bsz, n_slc, SEL_LEN, g, dk).transpose(0, 3, 1, 2, 4)
    nc = seq // SEL_Q_CHUNK
    qc = jnp.moveaxis(q.reshape(bsz, nc, SEL_Q_CHUNK, g, r, dk), 1, 0)
    sc = jnp.moveaxis(sel.reshape(bsz, nc, SEL_Q_CHUNK, g, n_top), 1, 0)
    b_idx = jnp.arange(bsz)[:, None, None, None]
    g_idx = jnp.arange(g)[None, None, :, None]
    scale = dk ** -0.5

    def chunk(args):
        q_c, sel_c, c = args
        t = c * SEL_Q_CHUNK + jnp.arange(SEL_Q_CHUNK)
        kg = kb[b_idx, g_idx, sel_c]
        vg = vb[b_idx, g_idx, sel_c]
        s = jnp.einsum("bcgrd,bcgkld->bcgrkl", q_c, kg, preferred_element_type=jnp.float32) * scale
        kpos = sel_c[..., None] * SEL_LEN + jnp.arange(SEL_LEN)
        mask = (kpos <= t[None, :, None, None, None])[:, :, :, None]
        flat = (bsz, SEL_Q_CHUNK, g, r, n_top * SEL_LEN)
        p = masked_softmax(s.reshape(flat), mask.reshape(bsz, SEL_Q_CHUNK, g, 1, n_top * SEL_LEN)).reshape(s.shape)
        return jnp.einsum("bcgrkl,bcgkld->bcgrd", p.astype(vg.dtype), vg)

    out = lax.map(chunk, (qc, sc, jnp.arange(nc)))
    return jnp.moveaxis(out, 0, 1).reshape(bsz, seq, g, r, dk)

def conformer_conv(u, conv_w, conv_b, ln_g, ln_b):
    a, gte = jnp.split(u, 2, axis=-1)
    c = a * jax.nn.sigmoid(gte)
    c = causal_depthwise_conv(c, conv_w, conv_b)
    return jax.nn.silu(layer_norm(c, ln_g, ln_b))

def pool_mixer(u, w, scale):
    bsz, seq, _ = u.shape
    uf = u.reshape(bsz, seq, POOL_GROUPS, POOL_GROUP_CH).astype(jnp.float32)
    cs = jnp.pad(jnp.cumsum(uf, axis=1), ((0, 0), (1, 0), (0, 0), (0, 0)))
    t = jnp.arange(seq)[:, None]
    win = jnp.array(POOL_WINDOWS, dtype=jnp.int32)[None, :]
    lo = jnp.maximum(t + 1 - win, 0)
    g_idx = jnp.arange(POOL_GROUPS)[None, :]
    mean = (cs[:, 1:] - cs[:, lo, g_idx]) / (t + 1 - lo).astype(jnp.float32)[None, :, :, None]
    pooled = (mean - uf).astype(u.dtype)
    mixed = jnp.einsum("bsgc,gcd->bsgd", pooled, w)
    return mixed.reshape(bsz, seq, POOL_CH) * scale

def second_inputs(seed: int = 0) -> dict:
    key = jax.random.key(seed)
    ks = jax.random.split(key, 24)
    f32 = jnp.float32
    L = DEPTH

    def nrm(k, shape, scale):
        return jax.random.normal(k, shape, f32) * scale

    return {
        "x": nrm(ks[0], (BATCH, SEQ, D_MODEL), 1.0),
        "norm_mix_pre": 1.0 + nrm(ks[1], (L, D_MODEL), 0.05),
        "norm_mix_post": 1.0 + nrm(ks[2], (L, D_MODEL), 0.05),
        "norm_ffn_pre": 1.0 + nrm(ks[3], (L, D_MODEL), 0.05),
        "norm_ffn_post": 1.0 + nrm(ks[4], (L, D_MODEL), 0.05),
        "w_in": nrm(ks[5], (L, D_MODEL, IN_COLS), D_MODEL ** -0.5),
        "nsa_cmp_pos": nrm(ks[6], (L, 2, CMP_LEN, HEAD_DIM), 0.1),
        "nsa_cmp_w1": nrm(ks[7], (L, 2, CMP_LEN * HEAD_DIM, CMP_HIDDEN), (CMP_LEN * HEAD_DIM) ** -0.5),
        "nsa_cmp_w2": nrm(ks[8], (L, 2, CMP_HIDDEN, HEAD_DIM), CMP_HIDDEN ** -0.5),
        "swa_sinks": nrm(ks[9], (L, SWA_HEADS), 0.5),
        "conv_w": nrm(ks[10], (L, CONV_WIDTH, CONV_CH), CONV_WIDTH ** -0.5),
        "conv_b": nrm(ks[11], (L, CONV_CH), 0.01),
        "conv_ln_g": 1.0 + nrm(ks[12], (L, CONV_CH), 0.05),
        "conv_ln_b": nrm(ks[13], (L, CONV_CH), 0.01),
        "pool_w": nrm(ks[14], (L, POOL_GROUPS, POOL_GROUP_CH, POOL_GROUP_CH), POOL_GROUP_CH ** -0.5),
        "pool_scale": 1.0 + nrm(ks[15], (L, POOL_CH), 0.1),
        "w_branch": nrm(ks[16], (L, N_BRANCH, BRANCH_W, D_MODEL), BRANCH_W ** -0.5),
        "w_gate": nrm(ks[17], (L, D_MODEL, N_BRANCH * D_MODEL), D_MODEL ** -0.5),
        "w_o": nrm(ks[18], (L, D_MODEL, D_MODEL), D_MODEL ** -0.5),
        "ffn_w_up": nrm(ks[19], (L, D_MODEL, 2 * D_FF_2), D_MODEL ** -0.5),
        "ffn_conv_w": nrm(ks[20], (L, FFN_CONV_WIDTH, 2 * D_FF_2), FFN_CONV_WIDTH ** -0.5),
        "ffn_conv_b": nrm(ks[21], (L, 2 * D_FF_2), 0.01),
        "ffn_w_down": nrm(ks[22], (L, D_FF_2, D_MODEL), D_FF_2 ** -0.5),
    }

def second_block(x, norm_mix_pre, norm_mix_post, norm_ffn_pre, norm_ffn_post, w_in,
              nsa_cmp_pos, nsa_cmp_w1, nsa_cmp_w2, swa_sinks, conv_w, conv_b, conv_ln_g,
              conv_ln_b, pool_w, pool_scale, w_branch, w_gate, w_o, ffn_w_up, ffn_conv_w,
              ffn_conv_b, ffn_w_down):
    bsz, seq, _ = x.shape
    cos, sin = rope_tables_2(seq)
    splits = np.cumsum(IN_SIZES)[:-1].tolist()
    for l in range(DEPTH):
        h = rms_norm_2(x, norm_mix_pre[l])
        proj = h @ w_in[l]
        a_q, a_kv, a_gate, d_q, d_kv, b_in, c_in = jnp.split(proj, splits, axis=-1)

        qa = a_q.reshape(bsz, seq, NSA_KV, NSA_R, HEAD_DIM)
        kv = a_kv.reshape(bsz, seq, 3, 2, NSA_KV, HEAD_DIM)
        k_cmp = nsa_compress(kv[:, :, 0, 0], nsa_cmp_pos[l, 0], nsa_cmp_w1[l, 0], nsa_cmp_w2[l, 0])
        v_cmp = nsa_compress(kv[:, :, 0, 1], nsa_cmp_pos[l, 1], nsa_cmp_w1[l, 1], nsa_cmp_w2[l, 1])
        o_cmp, p_cmp = nsa_compressed_attention(qa, k_cmp, v_cmp)
        sel = nsa_select_blocks(p_cmp, seq)
        qa_rot = apply_rope(qa, cos, sin)
        o_slc = nsa_selected_attention(qa_rot, apply_rope(kv[:, :, 1, 0], cos, sin), kv[:, :, 1, 1], sel)
        o_win = banded_attention(qa_rot, apply_rope(kv[:, :, 2, 0], cos, sin), kv[:, :, 2, 1], NSA_WINDOW, None)
        ga = jax.nn.sigmoid(a_gate).reshape(bsz, seq, 3, NSA_KV, NSA_R, 1)
        o_a = (ga[:, :, 0] * o_cmp + ga[:, :, 1] * o_slc + ga[:, :, 2] * o_win).reshape(bsz, seq, BRANCH_W)

        o_b = conformer_conv(b_in, conv_w[l], conv_b[l], conv_ln_g[l], conv_ln_b[l])

        o_c = pool_mixer(c_in, pool_w[l], pool_scale[l])

        qd = apply_rope(d_q.reshape(bsz, seq, SWA_KV, SWA_R, HEAD_DIM), cos, sin)
        kvd = d_kv.reshape(bsz, seq, 2, SWA_KV, HEAD_DIM)
        o_d = banded_attention(qd, apply_rope(kvd[:, :, 0], cos, sin), kvd[:, :, 1], SWA_WINDOW,
                               swa_sinks[l]).reshape(bsz, seq, BRANCH_W)

        branches = jnp.stack([o_a, o_b, o_c, o_d], axis=2)
        up = jnp.einsum("bsnc,ncd->bsnd", branches, w_branch[l])
        gates = jax.nn.sigmoid((h @ w_gate[l]).reshape(bsz, seq, N_BRANCH, D_MODEL))
        mix = jnp.einsum("bsnd,bsnd->bsd", gates, up) @ w_o[l]
        x = x + rms_norm_2(mix, norm_mix_post[l])

        hf = rms_norm_2(x, norm_ffn_pre[l])
        u = causal_depthwise_conv(hf @ ffn_w_up[l], ffn_conv_w[l], ffn_conv_b[l])
        gate, val = jnp.split(u, 2, axis=-1)
        f = (jax.nn.gelu(gate, approximate=True) * val) @ ffn_w_down[l]
        x = x + rms_norm_2(f, norm_ffn_post[l])
    return x


def setup_inputs(seed=0):
    out = dict(first_inputs(seed))
    for name, value in second_inputs(seed + 1).items():
        if name != "x":
            out[name + "_2"] = value
    return out


def reference(
    x, norm_ffn1, ffn1_w_gate, ffn1_w_up, ffn1_w_down, norm_mix, w_in, w_proj_dil, w_proj_sb,
    w_out, norm_ffn2, ffn2_w_gate, ffn2_w_up, ffn2_w_down, norm_final, norm_mix_pre_2,
    norm_mix_post_2, norm_ffn_pre_2, norm_ffn_post_2, w_in_2, nsa_cmp_pos_2, nsa_cmp_w1_2,
    nsa_cmp_w2_2, swa_sinks_2, conv_w_2, conv_b_2, conv_ln_g_2, conv_ln_b_2, pool_w_2,
    pool_scale_2, w_branch_2, w_gate_2, w_o_2, ffn_w_up_2, ffn_conv_w_2, ffn_conv_b_2,
    ffn_w_down_2,
):
    x = first_block(
        x, norm_ffn1, ffn1_w_gate, ffn1_w_up, ffn1_w_down, norm_mix, w_in, w_proj_dil,
        w_proj_sb, w_out, norm_ffn2, ffn2_w_gate, ffn2_w_up, ffn2_w_down, norm_final,
    )
    return second_block(
        x, norm_mix_pre_2, norm_mix_post_2, norm_ffn_pre_2, norm_ffn_post_2, w_in_2,
        nsa_cmp_pos_2, nsa_cmp_w1_2, nsa_cmp_w2_2, swa_sinks_2, conv_w_2, conv_b_2, conv_ln_g_2,
        conv_ln_b_2, pool_w_2, pool_scale_2, w_branch_2, w_gate_2, w_o_2, ffn_w_up_2,
        ffn_conv_w_2, ffn_conv_b_2, ffn_w_down_2,
    )


_drawn_inputs = setup_inputs


def setup_inputs(seed=0):
    import zlib

    import numpy as np

    out = dict(_drawn_inputs(seed))
    spreads = {}
    factors = {'swa_sinks_2': 5.754, 'conv_b_2': 4.17, 'conv_ln_b_2': 8.0, 'ffn_conv_b_2': 4.95}
    for name, (base, spread) in spreads.items():
        noise = np.random.default_rng([zlib.crc32(name.encode()), seed]).standard_normal(out[name].shape)
        drawn = base * np.exp(spread * noise) if base else spread * noise
        out[name] = jnp.asarray(drawn.astype(out[name].dtype))
    for name, factor in factors.items():
        out[name] = (out[name] * factor).astype(out[name].dtype)
    return out
```

```python
import numpy as np

import concourse.bass as bass
from concourse import mybir
from contextlib import ExitStack

F32 = mybir.dt.float32
F32R = mybir.dt.float32r
ALU = mybir.AluOpType
ACT = mybir.ActivationFunctionType
AX = mybir.AxisListType

P = 128
SEQ = 256
TT = SEQ // P
D = 1024
KC = D // P
DH = 64
FF = 2816
DEPTH = 2
EPS = 1e-6
BIG = 1e30
QSCALE = DH ** -0.5

ARENA = 12800
UNIT = 2048
UC = UNIT // KC
RING = 3
PAIRS = FF // UC
FFN_UNITS = 3 * PAIRS

M1_Q, M1_K, M1_V, M1_SBQ, M1_SBK, M1_SBV, M1_GATE, M1_PROJ, M1_OUT, M1_END = 0, 3, 6, 9, 10, 11, 12, 20, 22, 27
L1_UNITS = 2 * FFN_UNITS + M1_END
M2_Q, M2_CMP, M2_SLC, M2_WIN, M2_DQ, M2_DKV, M2_CONV, M2_POOL, M2_AG, M2_W1, M2_GATE, M2_OUT, M2_END = (
    0, 2, 3, 4, 5, 7, 8, 12, 14, 15, 19, 43, 48)
L2_UNITS = M2_END + FFN_UNITS
assert L1_UNITS % RING == 0 and L2_UNITS % RING == 0 and FFN_UNITS % RING == 0 and M2_END % RING == 0

G1_HEADS = 4
DILATION = ((128, 1), (512, 4), (2048, 16))
NG = len(DILATION)
SBH = 4

NSA_H = 8
SWA_JOBS = NSA_H // 2
KVH = 2
GRP = NSA_H // KVH
CMP_LEN, CMP_STRIDE, CMP_HID = 32, 16, 256
NCMP = (SEQ - CMP_LEN) // CMP_STRIDE + 1
CP = 16
CJ = CMP_LEN // 2
SWA_WINDOW = 128
CONVW = 31
CONV_PAD = CONVW - 1
POOL_PAD = 16
POOL_WINDOWS = (2, 4, 8, 16)
NBR = 4
BRC = 4

PAR_TILES = (120, 96, 124, 124, 88, 88, 88, 88)
PAR_START = tuple(sum(PAR_TILES[:i]) for i in range(len(PAR_TILES)))
PAR_COLS = sum(PAR_TILES)
C_FFN1, C_MIX, C_FFN2, C_FINAL, C_MIXPRE, C_MIXPOST, C_FFNPRE, C_FFNPOST = 0, 16, 32, 48, 56, 72, 88, 104
C_CONVB, C_LNG, C_LNB, C_POOLS, C_POS = 120, 128, 136, 144, 152
C_CONVW = PAR_START[2]
C_FCONV = PAR_START[4]
FCH = 2 * FF // P


SCORES_AT = (7, 9, 11, 13)
SB_AT = 15
JOB_AT = 15
JOBS = SWA_JOBS + NSA_H
CMP_AT = 19
POOL_AT = 16
CONV_FROM, CONV_STEPS = 13, 18
LN_AT = 31
BRANCH_ORDER = (2, 3, 1, 0)
FILLS = M2_W1 + NBR * 8
SB_STEPS = 5
N_SETUP = 5
N_SMALL = 5
SC_STEPS, SC_DEN = 4, 7
N_UPDATES = 3 * DEPTH + 2 + 2 * DEPTH


def layout(parts):
    at, n = {}, 0
    for name, size in parts:
        at[name] = n
        n += size
    return at, n


C1_AT, C1_N = layout([("cos", SEQ), ("sin", SEQ), ("rot", P), ("mask1", NG * SEQ), ("mask0", NG * P),
                      ("past", 3 * P), ("tri", P)])
C2_AT, C2_N = layout([("cos", SEQ), ("sin", SEQ), ("rot", P), ("dup", 2 * P), ("rotdup", 2 * P),
                      ("causal", 3 * P), ("window", 3 * P), ("cmpadd", TT * CP), ("cmp01", TT * CP),
                      ("blockdiag", P), ("inv", len(POOL_WINDOWS) * POOL_PAD)])


def rope_consts(theta, dims):
    half = dims // 2
    if theta == 500000.0:
        inv = (np.float32(theta) ** (-np.arange(0, dims, 2, dtype=np.float32) / np.float32(dims))).astype(np.float32)
    else:
        inv = (np.float32(1) / np.float32(theta) ** (np.arange(0, dims, 2, dtype=np.float32) / np.float32(dims))).astype(np.float32)
    ang = np.arange(SEQ, dtype=np.float32)[None, :] * inv[:, None]
    cos, sin = np.ones((P, SEQ), np.float32), np.zeros((P, SEQ), np.float32)
    rot = np.zeros((P, P), np.float32)
    for head in range(P // DH):
        for i in range(half):
            a, b = head * DH + i, head * DH + half + i
            cos[a] = cos[b] = np.cos(ang[i])
            sin[a] = sin[b] = np.sin(ang[i])
            rot[b, a], rot[a, b] = -1.0, 1.0
    return cos, sin, rot


def shape_consts():
    q, k = np.arange(SEQ)[:, None], np.arange(SEQ)[None, :]

    def tiles(ok):
        add = np.where(ok, 0.0, BIG).astype(np.float32)
        return add[:P, :P], add[P:, :]

    cos, sin, rot = rope_consts(500000.0, DH // 4)
    m = [tiles((k <= q) & ((q - k) % dil == 0) & (q - k <= win)) for win, dil in DILATION]
    past = (k < q).astype(np.float32).T
    tri = -(np.arange(P)[:, None] > np.arange(P)[None, :]).astype(np.float32)
    c1 = np.concatenate([cos, sin, rot, *(x[1] for x in m), *(x[0] for x in m), past[:P], past[P:, P:], tri], 1)

    cos, sin, rot = rope_consts(10000.0, DH)
    dup = [np.zeros((P, P), np.float32) for _ in range(KVH)]
    for g in range(KVH):
        for i in range(P):
            dup[g][g * DH + i % DH, i] = 1.0
    causal, window = tiles(k <= q), tiles((k <= q) & (k > q - SWA_WINDOW))
    n = np.arange(CP)[None, :]
    seen = (n * CMP_STRIDE + CMP_LEN - 1 <= q) & (n < NCMP)
    cmpadd = np.where(seen, 0.0, BIG).reshape(TT, P, CP).transpose(1, 0, 2).reshape(P, -1)
    cmp01 = seen.astype(np.float32).reshape(TT, P, CP).transpose(1, 0, 2).reshape(P, -1)
    r = np.arange(P)
    blockdiag = ((r[:, None] // CP) % KVH == r[None, :] // DH)
    t = np.arange(POOL_PAD)
    inv = np.concatenate([1.0 / np.minimum(t + 1, w) for w in POOL_WINDOWS])[None, :].repeat(P, 0)
    c2 = np.concatenate([cos, sin, rot, *dup, *(x @ rot for x in dup), *causal, *window, cmpadd, cmp01, blockdiag, inv], 1)
    return (np.eye(P, dtype=np.float32), np.ascontiguousarray(c1, np.float32), np.ascontiguousarray(c2, np.float32))


def hybrid_network(nc, A, ident_in, c1_in, c2_in, out):
    with ExitStack() as ctx:
        def sb(name, cols, dt=F32):
            return ctx.enter_context(nc.sbuf_tensor(name, [P, cols], dt))[:, :]

        def sem(name):
            return ctx.enter_context(nc.semaphore(name))

        def sems(name, n):
            return [sem(f"{name}{i}") for i in range(n)]

        def view(buf, **dims):
            names = " ".join(dims)
            return buf.rearrange(f"p ({names}) -> p {names}", **dims)

        raw = view(sb("raw", RING * UNIT), s=RING, n=UNIT)
        whi = view(sb("whi", RING * UNIT, F32R), s=RING, n=UNIT)
        wlo = view(sb("wlo", RING * UNIT, F32R), s=RING, n=UNIT)
        xT = view(sb("xT", KC * SEQ), c=KC, t=SEQ)
        hhi = view(sb("hhi", KC * SEQ, F32R), c=KC, t=SEQ)
        hlo = view(sb("hlo", KC * SEQ, F32R), c=KC, t=SEQ)
        sq = view(sb("sq", 4 * SEQ), c=4, t=SEQ)
        ssum = sb("ssum", SEQ)
        std = sb("std", SEQ + TT)
        rstd = sb("rstd", SEQ + TT)
        par = sb("par", PAR_COLS)
        ident = sb("ident", P)
        neg_ones = sb("neg_ones", P)
        zero_col = sb("zero_col", 1)
        ones = sb("ones", P)
        consts = sb("consts", max(C1_N, C2_N))
        zeros = sb("zeros", 512, mybir.dt.bfloat16)
        eps_col = sb("eps_col", 1)
        hidhi = view(sb("hidhi", 2 * 2 * SEQ, F32R), b=2, c=2, t=SEQ)
        hidlo = view(sb("hidlo", 2 * 2 * SEQ, F32R), b=2, c=2, t=SEQ)
        brhi = view(sb("brhi", 2 * BRC * SEQ, F32R), b=2, c=BRC, t=SEQ)
        brlo = view(sb("brlo", 2 * BRC * SEQ, F32R), b=2, c=BRC, t=SEQ)
        gates = view(sb("gates", 16 * SEQ), c=16, t=SEQ)
        arena = sb("arena", ARENA)
        ps = ctx.enter_context(nc.psum_tensor("ps", [P, 8, 512], F32))[:, :, :]

        rstd_b = rstd[:, 0:SEQ]

        def rstd_over(n):
            return rstd_b.unsqueeze(1).broadcast_to([P, n, SEQ])

        def carve(parts):
            at, n = layout(parts)
            assert n <= ARENA, (n, ARENA)
            return {name: arena[:, at[name]:at[name] + w] for name, w in parts}

        xtok = view(arena[:, 0:TT * D], t=TT, n=D)
        parrow = view(arena[:, TT * D:TT * D + len(PAR_TILES) * P], i=len(PAR_TILES), n=P)
        otok = view(arena[:, 0:TT * D], t=TT, n=D)
        ff = carve([("pad2", 2 * 2 * (SEQ + 2)), ("conv2", 2 * 2 * SEQ), ("act", 2 * SEQ), ("scaled", 2 * SEQ),
                    ("hid", 2 * SEQ)])
        pad2 = view(ff["pad2"], w=2, c=2, t=SEQ + 2)
        conv2 = view(ff["conv2"], w=2, c=2, t=SEQ)
        gate_sb = pad2[:, 0, :, 2:]
        act_out, scaled, hidf = ff["act"], ff["scaled"], ff["hid"]
        m1 = carve([("qk", 16 * SEQ), ("v", TT * D), ("s", 2 * NG * 3 * P), ("pt", 2 * 3 * P), ("mn", 4), ("den", 4),
                    ("rec", 4), ("ropec", 2 * SEQ), ("ropes", 2 * SEQ)])
        qk = view(m1["qk"], c=16, t=SEQ)
        vtok = view(m1["v"], t=TT, n=D)
        s1 = view(m1["s"], b=2, n=NG * 3 * P)
        pt1 = view(m1["pt"], b=2, n=3 * P)
        mixed1 = qk[:, 8:16, :]
        mn1, den1, rec1 = (view(m1[x], b=2, t=TT) for x in ("mn", "den", "rec"))
        SBN = SBH * 3 * P
        sb_a = m1["s"][:, 0:SBN]
        sb_b = m1["qk"][:, 0:SBN]

        m2 = carve([("mixed", KC * SEQ), ("qa", BRC * SEQ), ("qr", BRC * SEQ), ("dqr", BRC * SEQ), ("kd", 3 * KVH * SEQ),
                    ("vt", 3 * TT * P), ("s", 2 * 2 * 3 * P), ("pt", 2 * 3 * P), ("cpad", BRC * (CONV_PAD + SEQ)),
                    ("w2", 2 * DH), ("sinks", NSA_H), ("ghid", 2 * 2 * KVH * CP), ("kc", KVH * CP), ("vb", P),
                    ("sc", TT * P), ("ptc", TT * P), ("ga", TT * 3 * NSA_H), ("mnc", 16), ("denc", 16), ("recc", 16),
                    ("mn", 8), ("den", 8), ("rec", 8), ("dsk", 8), ("es", 8), ("fix", POOL_PAD)])
        mixed2 = view(m2["mixed"], c=KC, t=SEQ)
        conv_a = view(m2["mixed"][:, 0:BRC * SEQ], c=BRC, t=SEQ)
        ropec2 = view(m2["mixed"][:, BRC * SEQ:BRC * SEQ + 2 * SEQ], c=2, t=SEQ)
        ropes2 = view(m2["mixed"][:, BRC * SEQ + 2 * SEQ:], c=2, t=SEQ)
        qa, qr, dqr = (view(m2[x], c=BRC, t=SEQ) for x in ("qa", "qr", "dqr"))
        ln_sq = silu_out = qa
        ln_std, ln_rstd = m2["dqr"][:, 0:SEQ], m2["dqr"][:, SEQ:2 * SEQ]
        gated_tmp = view(m2["dqr"][:, 2 * SEQ:], c=2, t=SEQ)
        kd = view(m2["kd"], k=3, g=KVH, t=SEQ)
        vt = view(m2["vt"], k=3, t=TT, n=P)
        s2 = view(m2["s"], b=2, i=2, n=3 * P)
        ktmp = view(m2["s"][:, 0:3 * SEQ], k=3, t=SEQ)
        cmp_kv = view(m2["s"][:, 3 * SEQ:5 * SEQ], v=2, t=SEQ)
        pt2 = view(m2["pt"], i=2, n=3 * P)
        pool_w = view(m2["pt"][:, 0:4 * P], g=4, n=P)
        cpad = view(m2["cpad"], c=BRC, t=CONV_PAD + SEQ)
        blkf = view(m2["cpad"][:, 0:2 * CJ * 2 * NCMP], v=2, j=CJ, g=KVH, n=NCMP)
        blk_hi, blk_lo = (x.rearrange("p b c t -> p b (c t)")[:, :, 0:CJ * 2 * NCMP] for x in (hidhi, hidlo))
        conv_acc = sq
        w2v = view(m2["w2"], m=2, d=DH)
        w2k = view(m2["ptc"], m=2, copy=2, d=DH)
        neg_sinks = m2["sinks"]
        ghid = view(m2["ghid"], v=2, m=2, g=KVH, n=CP)
        kc_t = view(m2["kc"], g=KVH, n=CP)
        vb, ptc = m2["vb"], m2["ptc"]
        sc = view(m2["sc"], t=TT, h=NSA_H, n=CP)
        hid_rep = view(m2["sc"], m=2, r=GRP, x=KVH * CP)
        ga = view(m2["ga"], t=TT, n=3 * NSA_H)
        mnc, denc, recc = m2["mnc"], m2["denc"], m2["recc"]
        mn2, den2, rec2, dsk, es = (view(m2[x], b=2, t=TT, i=2) for x in ("mn", "den", "rec", "dsk", "es"))
        fix16 = m2["fix"]
        pool_flat = gates.rearrange("p c t -> p (c t)")
        PW = POOL_PAD + SEQ
        pool_u, pool_a, pool_b = (view(pool_flat[:, i * 4 * PW:(i + 1) * 4 * PW], g=4, t=PW) for i in range(3))
        gate_buf = gates.rearrange("p (b c) t -> p b c t", b=2)
        post = carve([("t", KC * SEQ), ("sq", KC * SEQ)])
        post_t, post_sq = view(post["t"], c=KC, t=SEQ), view(post["sq"], c=KC, t=SEQ)

        def table(at, name, n):
            return consts[:, at[name]:at[name] + n]

        cos1, sin1 = (table(C1_AT, x, SEQ).unsqueeze(1).broadcast_to([P, 2, SEQ]) for x in ("cos", "sin"))
        rot1 = table(C1_AT, "rot", P)
        mask1 = table(C1_AT, "mask1", NG * SEQ)
        mask0 = table(C1_AT, "mask0", NG * P)
        past = table(C1_AT, "past", 3 * P)
        past0 = past[:, 0:SEQ].unsqueeze(1).broadcast_to([P, SBH, SEQ])
        past1 = past[:, SEQ:].unsqueeze(1).broadcast_to([P, SBH, P])
        tri = table(C1_AT, "tri", P)
        cos2, sin2 = (table(C2_AT, x, SEQ).unsqueeze(1).broadcast_to([P, 2, SEQ]) for x in ("cos", "sin"))
        rot2 = table(C2_AT, "rot", P)
        dup, rotdup = (view(table(C2_AT, x, 2 * P), g=KVH, n=P) for x in ("dup", "rotdup"))
        causal, window = (table(C2_AT, x, 3 * P).unsqueeze(1).broadcast_to([P, 2, 3 * P]) for x in ("causal", "window"))
        cmpadd, cmp01 = (view(table(C2_AT, x, TT * CP), t=TT, n=CP) for x in ("cmpadd", "cmp01"))
        blockdiag = table(C2_AT, "blockdiag", P)
        inv_count = view(table(C2_AT, "inv", 4 * POOL_PAD), g=4, n=POOL_PAD)

        def par_rows(i, r, n, src):
            return parrow[r:r + n, i, :], src

        def chunks(name):
            return A[name].rearrange("l (c p) -> (l c) p", p=P)

        par_loads = [par_rows(0, r, DEPTH * KC, chunks(n)) for n, r in (
            ("norm_ffn1", C_FFN1), ("norm_mix", C_MIX), ("norm_ffn2", C_FFN2), ("norm_mix_pre_2", C_MIXPRE),
            ("norm_mix_post_2", C_MIXPOST), ("norm_ffn_pre_2", C_FFNPRE), ("norm_ffn_post_2", C_FFNPOST))]
        par_loads.append(par_rows(0, C_FINAL, KC, A["norm_final"].rearrange("(c p) -> c p", p=P)))
        par_loads += [par_rows(1, r - PAR_START[1], DEPTH * BRC, chunks(n)) for n, r in (
            ("conv_b_2", C_CONVB), ("conv_ln_g_2", C_LNG), ("conv_ln_b_2", C_LNB), ("pool_scale_2", C_POOLS))]
        par_loads.append(par_rows(1, C_POS - PAR_START[1], DEPTH * 2 * CJ,
                                  A["nsa_cmp_pos_2"].rearrange("l v (j h) d -> (l v j) (h d)", h=2)))
        for i in range(DEPTH):
            par_loads.append(par_rows(2 + i, 0, CONVW * BRC, A["conv_w_2"][i].rearrange("k (c p) -> (k c) p", p=P)))
            taps = A["ffn_conv_w_2"][i].rearrange("k (c p) -> (k c) p", p=P)
            par_loads.append(par_rows(4 + 2 * i, 0, 2 * FCH, taps[0:2 * FCH, :]))
            par_loads.append(par_rows(5 + 2 * i, 0, FCH, taps[2 * FCH:3 * FCH, :]))
            par_loads.append(par_rows(5 + 2 * i, FCH, FCH, A["ffn_conv_b_2"][i].rearrange("(c p) -> c p", p=P)))
        n_par = len(par_loads)

        def bank(b, a=0, n=512):
            return ps[:, b, a:a + n]

        def banks(b, n):
            return ps.rearrange("p b n -> p (b n)")[:, b * 512:b * 512 + n]

        def par_col(c):
            return par[:, bass.ds(c, 1)]

        raw_ready = sems("raw_ready", RING)
        hi_ready = sems("hi_ready", RING)
        lo_ready = sems("lo_ready", RING)
        used = sems("used", RING)
        x_in, par_in, ident_in_s, c1_in_s, c2_in_s, out_s = (
            sem(n) for n in ("x_in", "par_in", "ident_in", "c1_in", "c2_in", "out_s"))
        x_turned, par_turned, par_ready, out_turned, out_copied = (
            sem(n) for n in ("x_turned", "par_turned", "par_ready", "out_turned", "out_copied"))
        setup_done = sem("setup_done")
        x_updated = sem("x_updated")
        h_hi, h_ready = sem("h_hi"), sem("h_ready")
        sq_ready, ssum_step, stats_done, std_done, rstd_ready = (
            sem(n) for n in ("sq_ready", "ssum_step", "stats_done", "std_done", "rstd_ready"))
        acc_done = sem("acc_done")
        gate_taken, act_done, scaled_done, up_taken, hid_hi, hid_ready = (
            sem(n) for n in ("gate_taken", "act_done", "scaled_done", "up_taken", "hid_hi", "hid_ready"))
        (unit_taken, rot_done, cos_done, sin_done, rope_done, s_done, s_taken, min_done, p_done, rec_done, p_normed,
         t_done, pt_taken, pv_done, ob_hi, ob_ready, gate_on, sb_z, sb_abs, sb_exp, sb_ln, sb_step, sb_after, sb_w,
         sb_wm, sb_pv, wp_done, gated, y_done, y_hi, y_ready) = (sem("m1_" + n) for n in (
            "unit_taken rot_done cos_done sin_done rope_done s_done s_taken min_done p_done rec_done p_normed "
            "t_done pt_taken pv_done ob_hi ob_ready gate_on sb_z sb_abs sb_exp sb_ln sb_step sb_after sb_w "
            "sb_wm sb_pv wp_done gated y_done y_hi y_ready").split())

        (small_in, post_sq_ready, post_stats, post_std, post_rstd, post_step, pad_zero, conv_first, conv_gate, conv_up,
         taken2, rot2_done, rot2_taken, rot2_step, cos2_done, rope2_done, blk_ready, blk_hi_done, blk_split, gelu_done,
         kcvb_done, kcvb_taken, sc_half, sc_step, sc_exp, sc_den, sc_pt, ptc_taken, s2_done, s2_taken, mn2_step, p2_done,
         den2_step, rec2_done, p2_normed, t2_done, pt2_taken, pv2_done, ob2_hi, ob2_ready, cg_on, c_ready, conv_step,
         ln_mean, ln_cent, ln_sqd, ln_var, ln_stdd, ln_step, silu_done, ga_raw, ga_on, pads, pool_step, pooled, pool_mm,
         pool_hi, pool_lo, gates_on, br_done, gated2, y2_done, y2_hi, y2_ready) = (sem("m2_" + n) for n in (
            "small_in post_sq_ready post_stats post_std post_rstd post_step pad_zero conv_first conv_gate conv_up "
            "taken2 rot2_done rot2_taken rot2_step cos2_done rope2_done blk_ready blk_hi_done blk_split gelu_done "
            "kcvb_done kcvb_taken sc_half sc_step sc_exp sc_den sc_pt ptc_taken s2_done s2_taken mn2_step p2_done "
            "den2_step rec2_done p2_normed t2_done pt2_taken pv2_done ob2_hi ob2_ready cg_on c_ready conv_step "
            "ln_mean ln_cent ln_sqd ln_var ln_stdd ln_step silu_done ga_raw ga_on pads pool_step pooled pool_mm "
            "pool_hi pool_lo gates_on br_done gated2 y2_done y2_hi y2_ready").split())

        block = ctx.enter_context(nc.Block())

        def gate_unit_at(k, i):
            return M2_GATE + 6 * k + i

        def branch_units(k):
            return gate_unit_at(k, 4), gate_unit_at(k, 5)

        first_of, second_of = ({branch_units(k)[n]: k for k in range(NBR)} for n in range(2))

        def fill_of(i, dp=0):
            if i < M2_W1:
                return i
            k, j = divmod(i - M2_GATE, 6)
            return M2_W1 + 8 * k + (j if j < 4 else 4 + dp)

        TURNS = ((1, "q", 0), (2, "q", 1), (3, "cmp", 0), (4, "k", 0), (5, "k", 1), (6, "q", 2), (7, "q", 3), (8, "k", 2))
        K_UNITS = {M2_SLC: 0, M2_WIN: 1, M2_DKV: 2}
        OUTPUTS = {1: (1, 0), 3: (1, 2), SWA_JOBS + 3: (1, 0), SWA_JOBS + 7: (1, 2)}
        N_OUT = len(OUTPUTS)

        def score_unit(j):
            return JOB_AT + 2 * j

        job_scored = {score_unit(j): j for j in range(JOBS)}
        job_turned = {score_unit(j) + 2: j for j in range(JOBS)}

        TURN_OF_Q = [n for n, x in enumerate(TURNS) if x[1] == "q"]
        ROPES = [x for x in TURNS if x[1] != "cmp"]
        ROPE_OF_Q = [n for n, x in enumerate(ROPES) if x[1] == "q"]
        ROPE_OF_K = [n for n, x in enumerate(ROPES) if x[1] == "k"]

        def mn_steps(l, j):
            return l * (4 * SWA_JOBS + 2 * NSA_H) + 2 * j + 2 * min(j, SWA_JOBS)

        def p_steps(l, j):
            return l * (4 * JOBS + SWA_JOBS) + 4 * j + min(j, SWA_JOBS)

        def rec_steps(l, j):
            return 2 * (l * JOBS + j)

        def uses1(l, s):
            return l * (L1_UNITS // RING) + s // RING

        def uses2(l, s):
            return DEPTH * (L1_UNITS // RING) + l * (L2_UNITS // RING) + s // RING

        @block.sync
        def _(sp):
            def load(slot, n, uses, src):
                sp.wait_ge(lo_ready[slot], uses)
                sp.dma_start(raw[:, slot, 0:n].rearrange("p (k c) -> p k c", k=src.shape[1]), src) \
                    .then_inc(raw_ready[slot], 16)

            def block_of(w, l, r0, k, c0, n):
                return w.rearrange("l d c -> (l d) c")[bass.ds(l * w.shape[1] + r0, k * P), bass.ds(c0, n)] \
                    .rearrange("(k p) c -> p k c", p=P)

            def cols(w, l, c0, n=UC):
                return block_of(w, l, 0, KC, c0, n)

            def rows(w, l, r0, k):
                return block_of(w, l, r0, k, 0, D)

            def ffn(l, uses, s0, w_gate, up0, w_up, w_down):
                load(0, UNIT, uses(l, s0), cols(w_gate, l, 0))
                load(1, UNIT, uses(l, s0), cols(w_up, l, up0))
                with sp.Fori(1, PAIRS) as p:
                    load(2, UNIT, uses(l, s0) + p - 1, cols(w_gate, l, p * UC))
                    load(0, UNIT, uses(l, s0) + p, cols(w_up, l, up0 + p * UC))
                    load(1, UNIT, uses(l, s0) + p, rows(w_down, l, (p - 1) * UC, UC // P))
                load(2, UNIT, uses(l, s0) + PAIRS - 1, rows(w_down, l, (PAIRS - 1) * UC, UC // P))

            def out_proj(l, uses, s, w):
                r = 0
                for k in (2, 2, 2, 1, 1):
                    load(s % RING, k * D, uses(l, s), rows(w, l, r, k))
                    s, r = s + 1, r + k * P

            with sp.Fori(0, DEPTH) as l:
                ffn(l, uses1, 0, A["ffn1_w_gate"], 0, A["ffn1_w_up"], A["ffn1_w_down"])
                s0 = FFN_UNITS
                for i in range(M1_PROJ):
                    load((s0 + i) % RING, UNIT, uses1(l, s0 + i), cols(A["w_in"], l, i * UC))
                for i, w in ((M1_PROJ, "w_proj_dil"), (M1_PROJ + 1, "w_proj_sb")):
                    load((s0 + i) % RING, UNIT, uses1(l, s0 + i), rows(A[w], l, 0, UNIT // D))
                out_proj(l, uses1, s0 + M1_OUT, A["w_out"])
                ffn(l, uses1, s0 + M1_END, A["ffn2_w_gate"], 0, A["ffn2_w_up"], A["ffn2_w_down"])
            with sp.Fori(0, DEPTH) as l:
                s = 0
                for c0 in (*(i * UC for i in range(5)), *((NSA_H * DH + 768 + 24) + i * UC for i in range(9))):
                    load(s % RING, UNIT, uses2(l, s), cols(A["w_in_2"], l, c0))
                    s += 1
                load(s % RING, KC * 24, uses2(l, s), cols(A["w_in_2"], l, NSA_H * DH + 768, 24))
                s += 1
                for v in range(2):
                    for part in range(2):
                        src = A["nsa_cmp_w1_2"][bass.ds(l, 1), v, part * D:(part + 1) * D, :]
                        load(s % RING, UNIT, uses2(l, s), src.rearrange("a (j p) c -> p (a j) c", p=P))
                        s += 1
                for n in BRANCH_ORDER:
                    gate_w = A["w_gate_2"] if n else A["w_gate_2"].rearrange("l (k p) c -> (l k) p c", p=P)
                    for i in range(4):
                        src = gate_w[bass.ds(l * KC, KC), :, i * UC:(i + 1) * UC].rearrange("k p c -> p k c") if n == 0 else                             cols(gate_w, l, n * D + i * UC)
                        load(s % RING, UNIT, uses2(l, s), src)
                        s += 1
                    for i in range(2):
                        w = A["w_branch_2"].rearrange("l n d c -> (l n d) c")
                        src = w[bass.ds(l * (NBR * BRC * P) + (n * BRC * P + i * UC), UC), :]
                        load(s % RING, UNIT, uses2(l, s), src.rearrange("(k p) c -> p k c", p=P))
                        s += 1
                out_proj(l, uses2, s, A["w_o_2"])
                ffn(l, uses2, M2_END, A["ffn_w_up_2"], FF, A["ffn_w_up_2"], A["ffn_w_down_2"])
            for slot in range(2):
                sp.wait_ge(lo_ready[slot], uses2(DEPTH, 0))
                sp.dma_start(raw[:, slot, 0:P], ident_in).then_inc(raw_ready[slot], 16)

        @block.tensor
        def _(pe):
            def mm3(o, w_hi, w_lo, m_hi, m_lo, start, stop):
                pe.matmul(o, w_hi, m_hi, start=start, stop=False, skip_group_check=True)
                pe.matmul(o, w_hi, m_lo, start=False, stop=False, skip_group_check=True)
                return pe.matmul(o, w_lo, m_hi, start=False, stop=stop, skip_group_check=True)

            def unit_ready(slot, uses):
                pe.wait_ge(lo_ready[slot], uses + 1)

            def project(slot, half, o, h_wait=None):
                for k in range(KC):
                    if h_wait is not None:
                        pe.wait_ge(h_ready, h_wait + k + 1)
                    c = k * UC + half * P
                    last = mm3(o, whi[:, slot, c:c + P], wlo[:, slot, c:c + P], hhi[:, k, :], hlo[:, k, :],
                               k == 0, k == KC - 1)
                return last

            def project_tokens(slot, c0, n, width, o):
                for t in range(TT):
                    for k in range(KC):
                        c = k * width + c0
                        tok = slice(t * P, (t + 1) * P)
                        pe.matmul(o[:, t, :], hhi[:, k, tok], whi[:, slot, c:c + n], start=(k == 0), stop=False)
                        pe.matmul(o[:, t, :], hlo[:, k, tok], whi[:, slot, c:c + n], start=False, stop=False)
                        last = pe.matmul(o[:, t, :], hhi[:, k, tok], wlo[:, slot, c:c + n], start=False,
                                         stop=(k == KC - 1))
                return last

            def acc(c):
                return bank(4 + c // 2, (c % 2) * SEQ, SEQ)

            def norm_stats(n):
                pe.wait_ge(ssum_step, (n + 1) * (KC - 1))
                pe.matmul(bank(2, 0, SEQ), ones, ssum, start=True, stop=True)
                for t in range(TT):
                    last = pe.matmul(bank(2, SEQ + t, 1), ssum[:, t * P:(t + 1) * P], ones[:, 0:1], start=True, stop=True)
                last.then_inc(stats_done, 1)

            def ffn(uses, f, n, hn):
                fp = f * PAIRS
                pe.wait_ge(x_updated, KC * (n + 1))
                for b in range(4, 8):
                    pe.matmul(bank(b), zeros[:, 0:P], zeros[:, :], start=True, stop=False, skip_group_check=True)

                def column_block(slot, u, b, h_wait=None):
                    unit_ready(slot, u)
                    project(slot, 0, bank(b, 0, SEQ), h_wait)
                    project(slot, 1, bank(b, SEQ, SEQ)).then_inc(used[slot], 1)

                def down(slot, u, buf, done=False):
                    unit_ready(slot, u)
                    for c in range(KC):
                        for i in range(2):
                            w = slice(i * D + c * P, i * D + (c + 1) * P)
                            last = mm3(acc(c), whi[:, slot, w], wlo[:, slot, w], hidhi[:, buf, i, :], hidlo[:, buf, i, :],
                                       False, done and i == 1)
                        if done and c % 2 and c < KC - 1:
                            last.then_inc(acc_done, 1)
                    last.then_inc(used[slot], 1)

                column_block(0, uses(0), 0, KC * hn)
                norm_stats(n)
                column_block(1, uses(0), 1)
                with pe.Fori(0, (PAIRS - 1) // 2) as it:
                    for j in range(2):
                        p = it * 2 + (j + 1)
                        pe.wait_ge(gate_taken, fp + p)
                        column_block(2, uses(0) + p - 1, 0)
                        pe.wait_ge(up_taken, fp + p)
                        column_block(0, uses(0) + p, 1)
                        pe.wait_ge(hid_ready, fp + p)
                        down(1, uses(0) + p, j)
                pe.wait_ge(hid_ready, fp + PAIRS)
                down(2, uses(0) + PAIRS - 1, 0, True)

            def out_proj(uses, s, y_base):
                kc = 0
                for n in (2, 2, 2, 1, 1):
                    slot = s % RING
                    unit_ready(slot, uses(s))
                    pe.wait_ge(y_base[0], y_base[1] + kc + n)
                    for c in range(KC):
                        for i in range(n):
                            w = slice(i * D + c * P, i * D + (c + 1) * P)
                            last = mm3(acc(c), whi[:, slot, w], wlo[:, slot, w], hhi[:, kc + i, :], hlo[:, kc + i, :],
                                       kc + i == 0 and c % 2 == 0, kc + i == KC - 1)
                        if kc + n == KC and c % 2 and c < KC - 1:
                            last.then_inc(acc_done, 1)
                    last.then_inc(used[slot], 1)
                    s, kc = s + 1, kc + n

            pe.wait_ge(ident_in_s, 16)
            pe.wait_ge(x_in, 16)
            for c in range(KC):
                for t in range(TT):
                    last = pe.transpose(bank(4 + c // 2, (c % 2) * SEQ + t * P, P), xtok[:, t, c * P:(c + 1) * P], ident)
                last.then_inc(x_turned, 1)
            pe.wait_ge(par_in, 16 * n_par)
            for i, n in enumerate(PAR_TILES):
                pe.transpose(bank(i // 4, (i % 4) * P, n), parrow[0:n, i, :], ident[0:n, 0:n]).then_inc(par_turned, 1)
            pe.wait_ge(par_ready, len(PAR_TILES))
            pe.wait_ge(setup_done, N_SETUP)

            def mixer1(l):
                s0 = FFN_UNITS

                def u(i):
                    return uses1(l, s0 + i)

                def slot(i):
                    return (s0 + i) % RING

                def taken(i):
                    if i >= 2:
                        pe.wait_ge(unit_taken, l * M1_PROJ + i - 1)

                def rope(i):
                    pe.wait_ge(unit_taken, l * M1_PROJ + i + 1)
                    if i >= 1:
                        pe.wait_ge(sin_done, l * M1_V + i)
                    pe.matmul(bank(3), rot1, qk[:, 2 * i:2 * i + 2, :], start=True, stop=True).then_inc(rot_done, 1)

                def scores(hs):
                    pe.wait_ge(rope_done, (l + 1) * M1_V)
                    if hs:
                        pe.wait_ge(s_taken, l * 2 * G1_HEADS + 2 * hs)
                    for g in range(NG):
                        h = g * G1_HEADS + hs
                        lane = slice((h % 2) * DH, (h % 2) * DH + DH)
                        q, k = qk[lane, h // 2, :], qk[lane, M1_V + h // 2, :]
                        pe.matmul(banks(2, NG * SEQ)[:, g * SEQ:(g + 1) * SEQ], q[:, P:SEQ], k, start=True, stop=True)
                        last = pe.matmul(bank(4, g * P, P), q[:, 0:P], k[:, 0:P], start=True, stop=True)
                    last.then_inc(s_done, 1)

                def attend(hs):
                    pe.wait_ge(p_normed, l * 2 * G1_HEADS + 2 * (hs + 1))
                    p1 = s1[:, hs % 2, 0:NG * SEQ]
                    p0 = s1[:, hs % 2, NG * SEQ:]

                    def turn(g):
                        n = hs * NG + g
                        b = 5 + n % 2
                        if n >= 2:
                            pe.wait_ge(pt_taken, l * G1_HEADS * NG + n - 1)
                        pe.transpose(bank(b, 0, P), p0[:, g * P:(g + 1) * P], ident)
                        pe.transpose(bank(b, P, P), p1[:, g * SEQ:g * SEQ + P], ident)
                        pe.transpose(bank(b, 2 * P, P), p1[:, g * SEQ + P:(g + 1) * SEQ], ident).then_inc(t_done, 1)

                    def times_v(g):
                        n = hs * NG + g
                        pe.wait_ge(pt_taken, l * G1_HEADS * NG + n + 1)
                        h = g * G1_HEADS + hs
                        lane = slice((hs % 2) * DH, (hs % 2) * DH + DH)
                        o = bank(7, (hs // 2) * SEQ, SEQ)[lane, :]
                        v = slice(h * DH, (h + 1) * DH)
                        pe.matmul(o, vtok[:, 0, v], pt1[:, n % 2, 0:SEQ], start=(g == 0), stop=False)
                        pe.matmul(o[:, P:], vtok[:, 1, v], pt1[:, n % 2, SEQ:], start=False, stop=(g == NG - 1)) \
                            .then_inc(pv_done, 1)

                    turn(0)
                    turn(1)
                    times_v(0)
                    turn(2)
                    times_v(1)
                    times_v(2)

                def sb_scores():
                    pe.wait_ge(s_taken, (l + 1) * 2 * G1_HEADS)
                    for half in range(2):
                        if half:
                            pe.wait_ge(sb_z, l * 2 + 1)
                        lane = slice(half * DH, half * DH + DH)
                        for i in range(half, SBH, 2):
                            q, k = qk[lane, 12 + i // 2, :], qk[lane, 14 + i // 2, :]
                            pe.matmul(banks(2, SBH * SEQ)[:, i * SEQ:(i + 1) * SEQ], k[:, 0:P], q, start=True, stop=True)
                            last = pe.matmul(bank(4, i * P, P), k[:, P:], q[:, P:], start=True, stop=True)
                        last.then_inc(sb_z, 1)

                def sb_suffix_sums():
                    pe.wait_ge(sb_step, l * SB_STEPS + 4)
                    k0, k1 = sb_a[:, 0:SBH * SEQ], sb_a[:, SBH * SEQ:]
                    for b in range(2):
                        pe.matmul(bank(2 + b), tri, k0[:, b * 512:(b + 1) * 512], start=True, stop=False)
                        pe.matmul(bank(2 + b).rearrange("p (h t) -> p h t", h=2)[:, :, P:], neg_ones,
                                  k1[:, b * SEQ:(b + 1) * SEQ].rearrange("p (h t) -> p h t", h=2), start=False, stop=True)
                    pe.matmul(bank(4), tri, k1, start=True, stop=True).then_inc(sb_after, 1)

                def sb_times_v():
                    pe.wait_ge(sb_wm, l * 2 + 2)
                    for i in range(SBH):
                        lane = slice((i % 2) * DH, (i % 2) * DH + DH)
                        o = bank(5, (i // 2) * SEQ, SEQ)[lane, :]
                        v = slice((NG * G1_HEADS + i) * DH, (NG * G1_HEADS + i + 1) * DH)
                        pe.matmul(o, vtok[:, 0, v], sb_b[:, i * SEQ:(i + 1) * SEQ], start=True, stop=False)
                        last = pe.matmul(o[:, P:], vtok[:, 1, v], sb_b[:, SBH * SEQ + i * P:SBH * SEQ + (i + 1) * P],
                                         start=False, stop=True)
                    last.then_inc(sb_pv, 1)

                for i in range(M1_PROJ):
                    taken(i)
                    unit_ready(slot(i), u(i))
                    b = i % 2
                    if M1_V <= i < M1_SBQ or i == M1_SBV:
                        project_tokens(slot(i), 0, UC, UC, bank(b).rearrange("p (t n) -> p t n", t=TT)) \
                            .then_inc(used[slot(i)], 1)
                    else:
                        project(slot(i), 0, bank(b, 0, SEQ), KC * (3 * l + 1) if i == 0 else None)
                        project(slot(i), 1, bank(b, SEQ, SEQ)).then_inc(used[slot(i)], 1)
                    if i == 0:
                        norm_stats(3 * l + 1)
                    if 1 <= i <= M1_V:
                        rope(i - 1)
                    if i in SCORES_AT:
                        scores(SCORES_AT.index(i))
                    if i - 2 in SCORES_AT:
                        attend(SCORES_AT.index(i - 2))
                    if i == SB_AT:
                        sb_scores()
                    if i == SB_AT + 2:
                        sb_suffix_sums()
                    if i == SB_AT + 4:
                        sb_times_v()

                ja, jb = slot(M1_PROJ), slot(M1_PROJ + 1)
                unit_ready(ja, u(M1_PROJ))
                unit_ready(jb, u(M1_PROJ + 1))
                pe.wait_ge(unit_taken, (l + 1) * M1_PROJ)
                pe.wait_ge(ob_ready, (l + 1) * 2)
                for c in range(KC):
                    if c >= 2:
                        pe.wait_ge(gated, l * 2 * KC + 2 * (c - 1))
                    for br, j in ((0, ja), (1, jb)):
                        for i in range(2):
                            w = slice(i * D + c * P, i * D + (c + 1) * P)
                            last = mm3(bank(c % 2, br * SEQ, SEQ), whi[:, j, w], wlo[:, j, w], brhi[:, 0, 2 * br + i, :],
                                       brlo[:, 0, 2 * br + i, :], i == 0, i == 1)
                        if c == KC - 1:
                            last.then_inc(used[j], 1)
                        elif br == 1:
                            last.then_inc(wp_done, 1)
                out_proj(lambda s: uses1(l, s), s0 + M1_OUT, (y_ready, l * KC))

            with pe.Fori(0, DEPTH) as l:
                ffn(lambda s: uses1(l, s), 2 * l, 3 * l, 3 * l)
                mixer1(l)
                ffn(lambda s: uses1(l, FFN_UNITS + M1_END + s), 2 * l + 1, 3 * l + 2, 3 * l + 2)
            norm_stats(3 * DEPTH)
            def post_norm(m):
                for c in range(KC):
                    pe.wait_ge(post_sq_ready, m * (KC // 2) + c // 2 + 1)
                    last = pe.matmul(bank(2, 0, SEQ), ones, post_sq[:, c, :], start=(c == 0), stop=(c == KC - 1))
                last.then_inc(post_stats, 1)

            def mixer2(l):
                hn = 3 * DEPTH + 2 * l

                def u(i):
                    return uses2(l, i)

                def fill(i, dp=0):
                    f = fill_of(i, dp)
                    if f >= 2:
                        pe.wait_ge(taken2, l * FILLS + f - 1)
                    return f % 2

                def turn(n, kind, k):
                    unit = TURNS[n][0]
                    pe.wait_ge(taken2, l * FILLS + unit)
                    pe.wait_ge(rot2_taken, l * len(TURNS) + n)
                    if kind == "q":
                        src = qa[:, 2 * k:2 * k + 2, :] if k < 2 else dqr[:, 2 * k - 4:2 * k - 2, :]
                        last = pe.matmul(bank(4), rot2, src, start=True, stop=True)
                    else:
                        for b, m, src in ((3, dup, ktmp[:, k, :]), (4, rotdup, ktmp[:, k, :])) if kind == "k" else \
                                ((3, dup, cmp_kv[:, 0, :]), (4, dup, cmp_kv[:, 1, :])):
                            for g in range(KVH):
                                last = pe.matmul(bank(b, g * SEQ, SEQ), m[:, g, :], src, start=True, stop=True)
                    last.then_inc(rot2_done, 1)

                def scores(j):
                    if j == 0:
                        pe.wait_ge(rope2_done, (l + 1) * (len(TURNS) - 1))
                    else:
                        pe.wait_ge(s2_taken, l * JOBS + j)
                    for i in range(2):
                        h = 2 * j + i if j < SWA_JOBS else j - SWA_JOBS
                        lane = slice((h % 2) * DH, (h % 2) * DH + DH)
                        q = (dqr if j < SWA_JOBS else qr)[lane, h // 2, :]
                        k = kd[lane, 2 if j < SWA_JOBS else i, h // GRP, :]
                        pe.matmul(bank(2 + i, 0, P), q[:, 0:P], k[:, 0:P], start=True, stop=True)
                        last = pe.matmul(bank(2 + i, P, SEQ), q[:, P:], k, start=True, stop=True)
                    last.then_inc(s2_done, 1)

                def attend(j):
                    pe.wait_ge(p2_normed, (l * JOBS + j + 1) * 4)
                    if j == 0:
                        pe.wait_ge(pool_lo, (l + 1) * BRC)
                    for i in range(2):
                        src = s2[:, j % 2, i, :]
                        for n in range(3):
                            last = pe.transpose(bank(5 + i, n * P, P), src[:, n * P:(n + 1) * P], ident)
                    last.then_inc(t2_done, 1)
                    done = sum(x < j for x in OUTPUTS)
                    pe.wait_ge(ob2_ready, l * N_OUT + done)
                    pe.wait_ge(pt2_taken, l * JOBS + j + 1)
                    if j >= SWA_JOBS:
                        pe.wait_ge(ptc_taken, l + 1)
                    for i in range(2):
                        h = 2 * j + i if j < SWA_JOBS else j - SWA_JOBS
                        g, r = h // GRP, h % GRP
                        o = bank(7, (h // 2 % 2) * SEQ, SEQ)[(h % 2) * DH:(h % 2) * DH + DH, :]
                        kind = 2 if j < SWA_JOBS else i
                        lane = slice(g * DH, (g + 1) * DH)
                        first, final = (True, True) if j < SWA_JOBS else (False, i == 1)
                        if j >= SWA_JOBS and i == 0:
                            row = slice(r * KVH * CP, (r + 1) * KVH * CP)
                            pe.matmul(o, vb[row, lane], ptc[row, :], start=True, stop=False)
                            pe.wait_ge(pt2_taken, l * JOBS + j + 1)
                        pe.matmul(o, vt[:, kind, 0, lane], pt2[:, i, 0:SEQ], start=first, stop=False)
                        last = pe.matmul(o[:, P:], vt[:, kind, 1, lane], pt2[:, i, SEQ:], start=False, stop=final)
                    last.then_inc(pv2_done, 1)

                def compress(i):
                    v, part = divmod(i - M2_W1, 2)
                    if i == M2_W1:
                        pe.wait_ge(rot2_taken, (l + 1) * len(TURNS))
                        pe.wait_ge(blk_split, (l + 1) * 2)
                    slot = i % RING
                    unit_ready(slot, u(i))
                    for m in range(2):
                        for jl in range(CJ // 2):
                            j = part * (CJ // 2) + jl
                            w = slice(jl * CMP_HID + m * P, jl * CMP_HID + (m + 1) * P)
                            b = slice(j * KVH * NCMP, (j + 1) * KVH * NCMP)
                            last = mm3(bank(4, v * 64 + m * 32, KVH * NCMP), whi[:, slot, w], wlo[:, slot, w],
                                       blk_hi[:, v, b], blk_lo[:, v, b], j == 0 and m == 0, j == CJ - 1)
                    last.then_inc(used[slot], 1)

                def compressed():
                    pe.wait_ge(gelu_done, (l + 1) * 2)
                    pe.wait_ge(small_in, (l + 1) * 16 * N_SMALL)
                    for m in range(2):
                        pe.matmul(bank(4, 0, KVH * CP), w2k[:, m, :, :].rearrange("p c d -> p (c d)"),
                                  ghid[:, 0, m, :, :].rearrange("p g n -> p (g n)"), start=(m == 0), stop=(m == 1))
                    for m in range(2):
                        last = pe.matmul(bank(4, P, P), hid_rep[:, m, :, :].rearrange("p r x -> p (r x)"),
                                         w2v[:, m, :].unsqueeze(1).broadcast_to([P, KVH, DH]), start=(m == 0), stop=(m == 1))
                    last.then_inc(kcvb_done, 1)

                def compressed_scores():
                    pe.wait_ge(kcvb_taken, (l + 1) * 2)
                    for half in range(2):
                        if half:
                            pe.wait_ge(sc_half, l * 2 + 1)
                        lane = slice(half * DH, half * DH + DH)
                        for h in range(half, NSA_H, 2):
                            g, r = h // GRP, h % GRP
                            for t in range(TT):
                                last = pe.matmul(bank(4, SEQ + t * P + (r * KVH + g) * CP, CP), qa[lane, h // 2, t * P:(t + 1) * P],
                                                 kc_t[lane, g, :], start=True, stop=True)
                        last.then_inc(sc_half, 1)

                def compressed_turn():
                    pe.wait_ge(sc_den, (l + 1) * SC_DEN)
                    for t in range(TT):
                        last = pe.transpose(bank(4, t * P, P), sc[:, t, :, :].rearrange("p h n -> p (h n)"), ident)
                    last.then_inc(sc_pt, 1)

                def pool_mix():
                    pe.wait_ge(pooled, (l + 1) * 12)
                    pe.wait_ge(small_in, (l + 1) * 16 * N_SMALL)
                    for g in range(4):
                        last = pe.matmul(bank(5 + g // 2, (g % 2) * SEQ, SEQ), pool_w[:, g, :], pool_u[:, g, POOL_PAD:],
                                         start=True, stop=True)
                    last.then_inc(pool_mm, 1)

                def branch(k):
                    ia, ib = branch_units(k)
                    for i in (ia, ib):
                        unit_ready(i % RING, u(i))
                    buf = k % 2
                    if k == 0:
                        pe.wait_ge(pool_lo, (l + 1) * BRC)
                    elif k == 2:
                        pe.wait_ge(ln_step, (l + 1) * 3)
                    else:
                        pe.wait_ge(ob2_ready, l * N_OUT + (2 if k == 1 else 4))
                    for dp in range(KC // 2):
                        b = fill(ia, dp)
                        for i in range(2):
                            c = 2 * dp + i
                            for kc in range(BRC):
                                slot = (ia if kc < 2 else ib) % RING
                                w = slice((kc % 2) * D + c * P, (kc % 2) * D + (c + 1) * P)
                                last = mm3(bank(b, i * SEQ, SEQ), whi[:, slot, w], wlo[:, slot, w], brhi[:, buf, kc, :],
                                           brlo[:, buf, kc, :], kc == 0, kc == BRC - 1)
                                if dp == KC // 2 - 1 and i == 1 and kc % 2:
                                    last.then_inc(used[slot], 1)
                        if dp < KC // 2 - 1:
                            last.then_inc(br_done, 1)

                for i in range(M2_OUT):
                    if i in second_of:
                        branch(second_of[i])
                    elif i in first_of:
                        pass
                    elif M2_W1 <= i < M2_GATE:
                        compress(i)
                    else:
                        b = fill(i)
                        slot = i % RING
                        unit_ready(slot, u(i))
                        if i == M2_AG:
                            project_tokens(slot, 0, 24, 24, bank(b, 0, TT * 24).rearrange("p (t n) -> p t n", t=TT)) \
                                .then_inc(used[slot], 1)
                        else:
                            project(slot, 0, bank(b, 0, SEQ), KC * hn if i == 0 else None)
                            if i in K_UNITS:
                                last = project_tokens(slot, P, P, UC, bank(b, SEQ, SEQ).rearrange("p (t n) -> p t n", t=TT))
                            else:
                                last = project(slot, 1, bank(b, SEQ, SEQ))
                            last.then_inc(used[slot], 1)
                    if i == 0:
                        norm_stats(3 * DEPTH + 1 + 2 * l)
                    for n, (unit, kind, k) in enumerate(TURNS):
                        if unit == i:
                            turn(n, kind, k)
                    if i == POOL_AT:
                        pool_mix()
                    if i in job_scored:
                        scores(job_scored[i])
                    if i == CMP_AT:
                        compressed()
                    if i == CMP_AT + 1:
                        compressed_scores()
                    if i == CMP_AT + 4:
                        compressed_turn()
                    if i == LN_AT:
                        pe.wait_ge(conv_step, (l + 1) * CONVW * BRC)
                        for c in range(BRC):
                            last = pe.matmul(bank(4, 0, SEQ), ones, conv_acc[:, c, :], start=(c == 0), stop=(c == BRC - 1))
                        last.then_inc(ln_mean, 1)
                    if i == LN_AT + 1:
                        pe.wait_ge(ln_sqd, l + 1)
                        for c in range(BRC):
                            last = pe.matmul(bank(4, SEQ, SEQ), ones, ln_sq[:, c, :], start=(c == 0), stop=(c == BRC - 1))
                        last.then_inc(ln_var, 1)
                    if i in job_turned:
                        attend(job_turned[i])
                out_proj(lambda s: uses2(l, s), M2_OUT, (y2_ready, l * KC))

            pe.wait_ge(c2_in_s, 16)
            with pe.Fori(0, DEPTH) as l:
                mixer2(l)
                post_norm(2 * l)
                ffn(lambda s: uses2(l, M2_END + s), 2 * DEPTH + l, 3 * DEPTH + 2 + 2 * l, 3 * DEPTH + 1 + 2 * l)
                post_norm(2 * l + 1)
            pe.wait_ge(x_updated, KC * N_UPDATES)
            for t in range(TT):
                for c in range(KC):
                    last = pe.transpose(bank(2 * t + c // 4, (c % 4) * P, P), xT[:, c, t * P:(t + 1) * P], ident)
                    if c % 4 == 3:
                        last.then_inc(out_turned, 1)

        @block.scalar
        def _(act):
            act.dma_start(xtok, A["x"].rearrange("b (t p) d -> p (b t) d", p=P)).then_inc(x_in, 16)
            act.dma_start(ident, ident_in).then_inc(ident_in_s, 16)
            for dst, src in par_loads:
                act.dma_start(dst, src).then_inc(par_in, 16)
            act.dma_start(consts[:, 0:C1_N], c1_in).then_inc(c1_in_s, 16)

            def split_hi(slot, uses, n=UNIT):
                act.wait_ge(raw_ready[slot], 16 * uses + 16)
                act.wait_ge(used[slot], uses)
                act.activation(whi[:, slot, 0:n], raw[:, slot, 0:n], ACT.Copy).then_inc(hi_ready[slot], 1)

            def norm_squares(n, c):
                if c >= 4:
                    act.wait_ge(ssum_step, n * (KC - 1) + max(1, c - 4))
                act.activation(sq[:, c % 4, :], xT[:, c, :], ACT.Square).then_inc(sq_ready, 1)

            def enter_norm(n, gain):
                for c in range(KC):
                    act.wait_ge(x_updated, KC * n + c + 1)
                    act.activation(hhi[:, c, :], xT[:, c, :], ACT.Copy, scale=par_col(gain + c)).then_inc(h_hi, 1)
                    norm_squares(n, c)

            def norm_std(n):
                act.wait_ge(stats_done, n + 1)
                act.activation(std, bank(2, 0, SEQ + TT), ACT.Sqrt, bias=eps_col).then_inc(std_done, 1)

            def ffn(uses, f, n, gain):
                fp = f * PAIRS
                enter_norm(n, gain)
                split_hi(2, uses(0))
                norm_std(n)

                def activate(p):
                    act.wait_ge(gate_taken, fp + p + 1)
                    act.wait_ge(scaled_done, fp + p)
                    act.activation(act_out, gate_sb, ACT.Silu).then_inc(act_done, 1)

                def hidden_hi(p, buf):
                    act.wait_ge(up_taken, fp + p + 1)
                    act.activation(hidhi[:, buf, :, :], hidf, ACT.Copy).then_inc(hid_hi, 1)

                activate(0)
                split_hi(0, uses(0) + 1)
                hidden_hi(0, 0)
                with act.Fori(0, (PAIRS - 1) // 2) as it:
                    for j in range(2):
                        p = it * 2 + (j + 1)
                        split_hi(1, uses(0) + p)
                        activate(p)
                        split_hi(2, uses(0) + p)
                        split_hi(0, uses(0) + p + 1)
                        hidden_hi(p, (j + 1) % 2)
                split_hi(1, uses(0) + PAIRS)

            act.wait_ge(setup_done, N_SETUP)
            for i, n in enumerate(PAR_TILES):
                act.wait_ge(par_turned, i // 4 * 4 + 4)
                act.activation(par[:, PAR_START[i]:PAR_START[i] + n], bank(i // 4, (i % 4) * P, n), ACT.Copy) \
                    .then_inc(par_ready, 1)
            act.wait_ge(par_ready, len(PAR_TILES))
            split_hi(0, 0)
            split_hi(1, 0)

            def mixer1(l):
                s0 = FFN_UNITS

                def next_split(i):
                    s = s0 + i + 2
                    n = D if i + 2 in (M1_OUT + 3, M1_OUT + 4) else UNIT
                    split_hi(s % RING, uses1(l, s), n)

                def probabilities(hs):
                    b = hs % 2
                    n = l * G1_HEADS + hs
                    for t, part in ((1, s1[:, b, 0:NG * SEQ]), (0, s1[:, b, NG * SEQ:])):
                        act.wait_ge(min_done, 2 * n + 2 - t)
                        if hs >= 2 and t == 1:
                            act.wait_ge(rec_done, n - 1)
                        act.activation(part, part, ACT.Exp, bias=mn1[:, b, t:t + 1], scale=-1.0,
                                       accum_out=den1[:, b, t:t + 1]).then_inc(p_done, 1)

                def turned(hs):
                    for g in range(NG):
                        n = l * G1_HEADS * NG + hs * NG + g
                        act.wait_ge(t_done, n + 1)
                        if hs * NG + g >= 2:
                            act.wait_ge(pv_done, n - 1)
                        m = (hs * NG + g) % 2
                        act.activation(pt1[:, m, :], bank(5 + m, 0, 3 * P), ACT.Copy).then_inc(pt_taken, 1)

                enter_norm(3 * l + 1, C_MIX + KC * l)
                for i in range(M1_PROJ):
                    next_split(i)
                    if i == 0:
                        norm_std(3 * l + 1)
                    if i - 3 in SCORES_AT:
                        turned(SCORES_AT.index(i - 3))
                    if i - 1 in SCORES_AT:
                        probabilities(SCORES_AT.index(i - 1))
                    if i == SB_AT + 1:
                        act.wait_ge(pv_done, (l + 1) * G1_HEADS * NG)
                        act.activation(brhi[:, 0, 0:2, :], bank(7), ACT.Copy).then_inc(ob_hi, 1)
                        act.wait_ge(sb_z, l * 2 + 2)
                        act.activation(sb_a, banks(2, SBN), ACT.Abs).then_inc(sb_abs, 1)
                        act.wait_ge(sb_abs, l + 1)
                        act.activation(sb_a, sb_a, ACT.Exp, scale=-1.0).then_inc(sb_exp, 1)
                        act.wait_ge(sb_exp, l + 1)
                        act.activation(sb_a, sb_a, ACT.Ln, bias=1.0).then_inc(sb_ln, 1)
                    if i == SB_AT + 3:
                        act.wait_ge(sb_step, l * SB_STEPS + 5)
                        act.activation(sb_b, sb_b, ACT.Exp).then_inc(sb_w, 1)
                    if i == M1_PROJ - 1:
                        for g in range(M1_GATE, i):
                            gate_unit(l, g)
                next_split(M1_PROJ)
                gate_unit(l, M1_PROJ - 1)
                act.wait_ge(sb_pv, l + 1)
                act.activation(brhi[:, 0, 2:4, :], bank(5), ACT.Copy).then_inc(ob_hi, 1)
                for c in range(KC):
                    act.wait_ge(y_done, l * KC + c + 1)
                    act.activation(hhi[:, c, :], mixed1[:, c, :], ACT.Copy).then_inc(y_hi, 1)
                for i in range(M1_PROJ + 1, M1_END):
                    next_split(i)

            def gate_unit(l, i):
                act.wait_ge(unit_taken, l * M1_PROJ + i + 1)
                part = gates[:, 2 * (i - M1_GATE):2 * (i - M1_GATE) + 2, :]
                act.activation(part, part, ACT.Sigmoid).then_inc(gate_on, 1)

            act.wait_ge(c1_in_s, 16)
            with act.Fori(0, DEPTH) as l:
                ffn(lambda s: uses1(l, s), 2 * l, 3 * l, C_FFN1 + KC * l)
                mixer1(l)
                ffn(lambda s: uses1(l, FFN_UNITS + M1_END + s), 2 * l + 1, 3 * l + 2, C_FFN2 + KC * l)
            for c in range(KC):
                act.wait_ge(x_updated, KC * 3 * DEPTH + c + 1)
                norm_squares(3 * DEPTH, c)
            act.dma_start(consts[:, 0:C2_N], c2_in).then_inc(c2_in_s, 16)
            norm_std(3 * DEPTH)

            def post_norm(m, a, slot, u):
                for b in range(KC // 2):
                    if b < KC // 2 - 1:
                        act.wait_ge(acc_done, a * (KC // 2 - 1) + b + 1)
                    else:
                        act.wait_ge(used[slot], u + 1)
                    act.activation(post_sq[:, 2 * b:2 * b + 2, :], bank(4 + b), ACT.Square).then_inc(post_sq_ready, 1)
                act.wait_ge(post_stats, m + 1)
                act.activation(std[:, 0:SEQ], bank(2, 0, SEQ), ACT.Sqrt, bias=eps_col).then_inc(post_std, 1)

            def ffn_conv(uses, l):
                fp = (2 * DEPTH + l) * PAIRS
                cp = l * PAIRS
                n = 3 * DEPTH + 2 + 2 * l
                enter_norm(n, C_FFNPRE + KC * l)
                split_hi(2, uses(0))
                norm_std(n)

                def last_tap(p, w):
                    act.wait_ge((gate_taken, up_taken)[w], fp + p + 1)
                    act.wait_ge(scaled_done, fp + p)
                    for c in range(2):
                        ch = C_FCONV + l * (4 * FCH) + w * (FCH // 2) + p * 2 + c
                        act.activation(conv2[:, w, c, :], pad2[:, w, c, 2:], ACT.Identity, scale=par_col(ch + 2 * FCH),
                                       bias=par_col(ch + 3 * FCH)).then_inc(conv_first, 1)

                def gelu(p):
                    act.wait_ge(conv_gate, (cp + p + 1) * 4)
                    act.activation(act_out, conv2[:, 0, :, :], ACT.Gelu_apprx_tanh).then_inc(act_done, 1)

                def hidden_hi(p, buf):
                    act.wait_ge(scaled_done, fp + p + 1)
                    act.activation(hidhi[:, buf, :, :], hidf, ACT.Copy).then_inc(hid_hi, 1)

                last_tap(0, 0)
                last_tap(0, 1)
                gelu(0)
                split_hi(0, uses(0) + 1)
                hidden_hi(0, 0)
                with act.Fori(0, (PAIRS - 1) // 2) as it:
                    for j in range(2):
                        p = it * 2 + (j + 1)
                        split_hi(1, uses(0) + p)
                        last_tap(p, 0)
                        split_hi(2, uses(0) + p)
                        last_tap(p, 1)
                        gelu(p)
                        split_hi(0, uses(0) + p + 1)
                        hidden_hi(p, (j + 1) % 2)
                split_hi(1, uses(0) + PAIRS)

            def mixer2(l):
                def next_split(i):
                    n = {M2_AG: KC * 24, M2_OUT + 3: D, M2_OUT + 4: D}.get(i + 2, UNIT)
                    split_hi((i + 2) % RING, uses2(l, i + 2), n)

                def probabilities(j):
                    n = l * JOBS + j
                    b = j % 2
                    act.wait_ge(mn2_step, mn_steps(l, j + 1))
                    for i in range(2):
                        for t, part in ((0, slice(0, P)), (1, slice(P, 3 * P))):
                            x = s2[:, b, i, part]
                            act.activation(x, x, ACT.Exp, bias=mn2[:, b, t, i:i + 1], scale=-1.0,
                                           accum_out=den2[:, b, t, i:i + 1]).then_inc(p2_done, 1)
                    if j < SWA_JOBS:
                        act.activation(es[:, b, :, :], dsk[:, b, :, :], ACT.Exp).then_inc(p2_done, 1)

                def turned(j):
                    act.wait_ge(t2_done, l * JOBS + j + 1)
                    act.activation(pt2, ps[:, 5:7, 0:3 * P], ACT.Copy).then_inc(pt2_taken, 1)

                def out_hi(j):
                    n = sorted(OUTPUTS).index(j)
                    buf, c = OUTPUTS[j]
                    act.wait_ge(pv2_done, l * JOBS + j + 1)
                    if j >= SWA_JOBS:
                        act.wait_ge(used[branch_units(1)[1] % RING], uses2(l, branch_units(1)[1]) + 1)
                    act.activation(brhi[:, buf, c:c + 2, :], bank(7), ACT.Copy).then_inc(ob2_hi, 1)

                for v, dst in ((0, w2k[:, :, 0, :]), (0, w2k[:, :, 1, :]), (1, w2v)):
                    src = A["nsa_cmp_w2_2"][bass.ds(l, 1), v]
                    act.dma_start(dst, src.rearrange("a (m p) d -> p (a m) d", p=P)).then_inc(small_in, 16)
                act.dma_start(pool_w, A["pool_w_2"][bass.ds(l, 1)].rearrange("a g c d -> c (a g) d")).then_inc(small_in, 16)
                act.dma_start(neg_sinks, A["swa_sinks_2"][bass.ds(l, 1), :].broadcast_to([P, NSA_H])).then_inc(small_in, 16)
                n = 3 * DEPTH + 1 + 2 * l
                enter_norm(n, C_MIXPRE + KC * l)
                for i in range(M2_OUT):
                    joint = i in second_of
                    if i - 1 in job_turned:
                        turned(job_turned[i - 1])
                    if not joint:
                        next_split(i)
                    if i == 0:
                        norm_std(n)
                    if i == 5:
                        for v in range(2):
                            act.wait_ge(blk_ready, l * 8 + 4 * v + 4)
                            act.activation(blk_hi[:, v, :], blkf[:, v, :, :, :].rearrange("p j g n -> p (j g n)"), ACT.Copy) \
                                .then_inc(blk_hi_done, 1)
                    if i == M2_POOL:
                        act.wait_ge(taken2, l * FILLS + M2_POOL)
                        x = cpad[:, :, CONV_PAD:]
                        act.activation(x, x, ACT.Sigmoid).then_inc(cg_on, 1)
                    if i == M2_AG + 1:
                        act.wait_ge(taken2, l * FILLS + M2_AG + 1)
                        act.activation(ga, ga, ACT.Sigmoid).then_inc(ga_on, 1)
                    if i == POOL_AT + 1:
                        act.wait_ge(pool_mm, l + 1)
                        for g in range(4):
                            act.activation(brhi[:, 0, g, :], bank(5 + g // 2, (g % 2) * SEQ, SEQ), ACT.Copy,
                                           scale=par_col(C_POOLS + BRC * l + g)).then_inc(pool_hi, 1)
                    if i == CMP_AT:
                        act.wait_ge(used[(CMP_AT - 1) % RING], uses2(l, CMP_AT - 1) + 1)
                        act.activation(ghid.rearrange("p v m g n -> p (v m) g n")[:, :, :, 0:NCMP],
                                       bank(4, 0, P).rearrange("p (x n) -> p x n", x=4)[:, :, 0:KVH * NCMP]
                                       .rearrange("p x (g n) -> p x g n", g=KVH), ACT.Gelu_apprx_tanh).then_inc(gelu_done, 1)
                        act.wait_ge(gelu_done, l * 2 + 1)
                        act.wait_ge(pads, l * 3 + 2)
                        act.activation(hid_rep, ghid[:, 1, :, :, :].rearrange("p m g n -> p m (g n)").unsqueeze(2)
                                       .broadcast_to([P, 2, GRP, KVH * CP]), ACT.Copy).then_inc(gelu_done, 1)
                    if i == CMP_AT + 2:
                        act.wait_ge(sc_step, l * SC_STEPS + 4)
                        act.activation(sc, sc, ACT.Exp, scale=-1.0).then_inc(sc_exp, 1)
                    if i == CMP_AT + 5:
                        act.wait_ge(sc_pt, l + 1)
                        act.activation(ptc, bank(4, 0, TT * P), ACT.Copy).then_inc(ptc_taken, 1)
                    if i - 1 in job_scored:
                        probabilities(job_scored[i - 1])
                    if i - 1 in job_turned and job_turned[i - 1] in OUTPUTS:
                        out_hi(job_turned[i - 1])
                    if i in first_of:
                        k = first_of[i]
                        act.wait_ge(taken2, l * FILLS + fill_of(gate_unit_at(k, 3)) + 1)
                        x = gate_buf[:, k % 2, :, :]
                        act.activation(x, x, ACT.Sigmoid).then_inc(gates_on, 1)
                    if i == LN_AT + 1:
                        act.wait_ge(ln_cent, l + 1)
                        act.activation(ln_sq, conv_acc, ACT.Square).then_inc(ln_sqd, 1)
                    if i == LN_AT + 2:
                        act.wait_ge(ln_var, l + 1)
                        act.activation(ln_std, bank(4, SEQ, SEQ), ACT.Sqrt, scale=2.0, bias=eps_col).then_inc(ln_stdd, 1)
                    if i == LN_AT + 3:
                        act.wait_ge(ln_step, l * 3 + 2)
                        for c in range(BRC):
                            act.activation(silu_out[:, c, :], conv_acc[:, c, :], ACT.Silu, scale=par_col(C_LNG + BRC * l + c),
                                           bias=par_col(C_LNB + BRC * l + c)).then_inc(silu_done, 1)
                        act.wait_ge(silu_done, (l + 1) * 5 - 1)
                        act.activation(brhi[:, 0, :, :], silu_out, ACT.Copy).then_inc(silu_done, 1)
                    if joint:
                        if second_of[i] == NBR - 1:
                            for c in range(KC // 2):
                                act.wait_ge(y2_done, l * (KC // 2) + c + 1)
                                act.activation(hhi[:, 2 * c:2 * c + 2, :], mixed2[:, 2 * c:2 * c + 2, :], ACT.Copy).then_inc(y2_hi, 1)
                        next_split(i)
                for i in range(M2_OUT, M2_END):
                    next_split(i)

            with act.Fori(0, DEPTH) as l:
                mixer2(l)
                post_norm(2 * l, 3 * DEPTH + 2 * l, (M2_END - 1) % RING, uses2(l, M2_END - 1))
                ffn_conv(lambda s: uses2(l, M2_END + s), l)
                post_norm(2 * l + 1, 3 * DEPTH + 2 * l + 1, 2, uses2(l, M2_END) + PAIRS - 1)
            for t in range(TT):
                act.wait_ge(out_copied, 2 * t + 2)
                act.dma_start(out[0, t * P:(t + 1) * P, :], otok[:, t, :]).then_inc(out_s, 16)
            act.wait_ge(out_s, 16 * TT)

        @block.gpsimd
        def _(pool):
            pool.memset(ones, 1.0 / D).then_inc(setup_done, 1)
            pool.memset(zeros, 0.0).then_inc(setup_done, 1)
            pool.memset(eps_col, EPS).then_inc(setup_done, 1)
            pool.memset(neg_ones, -1.0).then_inc(setup_done, 1)
            pool.memset(zero_col, 0.0).then_inc(setup_done, 1)

            def sum_squares(n):
                for c in range(1, KC):
                    pool.wait_ge(sq_ready, KC * n + c + 1)
                    if c > 1:
                        pool.wait_ge(ssum_step, n * (KC - 1) + c - 1)
                    pool.tensor_tensor(ssum, sq[:, 0, :] if c == 1 else ssum, sq[:, c % 4, :], ALU.add) \
                        .then_inc(ssum_step, 1)

            def ffn(f, n):
                fp = f * PAIRS
                sum_squares(n)

                with pool.Fori(0, PAIRS) as p:
                    pool.wait_ge(act_done, fp + p + 1)
                    pool.wait_ge(up_taken, fp + p)
                    pool.tensor_tensor(scaled.rearrange("p (c t) -> p c t", c=2), act_out.rearrange("p (c t) -> p c t", c=2),
                                       rstd_over(2), ALU.mult).then_inc(scaled_done, 1)

            def mixer1(l):
                sum_squares(3 * l + 1)
                for i in range(M1_V):
                    pool.wait_ge(unit_taken, l * M1_PROJ + i + 1)
                    if i >= 1:
                        pool.wait_ge(rope_done, l * M1_V + i)
                    pool.tensor_tensor(m1["ropec"].rearrange("p (c t) -> p c t", c=2), qk[:, 2 * i:2 * i + 2, :], cos1,
                                       ALU.mult).then_inc(cos_done, 1)
                for hs in range(G1_HEADS):
                    n = l * G1_HEADS + hs
                    pool.wait_ge(rec_done, n + 1)
                    for t, part in ((1, s1[:, hs % 2, 0:NG * SEQ]), (0, s1[:, hs % 2, NG * SEQ:])):
                        rec = rec1[:, hs % 2, t:t + 1].broadcast_to([P, part.shape[1]])
                        pool.tensor_tensor(part, part, rec, ALU.mult).then_inc(p_normed, 1)
                pool.wait_ge(sb_w, l + 1)
                w0 = sb_b[:, 0:SBH * SEQ].rearrange("p (h t) -> p h t", h=SBH)
                w1 = sb_b[:, SBH * SEQ:].rearrange("p (h t) -> p h t", h=SBH)
                pool.tensor_tensor(w0, w0, past0, ALU.mult).then_inc(sb_wm, 1)
                pool.tensor_tensor(w1, w1, past1, ALU.mult).then_inc(sb_wm, 1)

            with pool.Fori(0, DEPTH) as l:
                ffn(2 * l, 3 * l)
                mixer1(l)
                ffn(2 * l + 1, 3 * l + 2)
            sum_squares(3 * DEPTH)

            def zero(dst, done):
                column = zero_col.unsqueeze(2).broadcast_to(dst.shape)
                pool.tensor_tensor(dst, column, column, ALU.add).then_inc(done, 1)

            def ffn_conv(l):
                fp = (2 * DEPTH + l) * PAIRS
                sum_squares(3 * DEPTH + 2 + 2 * l)
                zero(pad2[:, :, :, 0:2].rearrange("p w c t -> p (w c) t"), pad_zero)
                with pool.Fori(0, PAIRS) as p:
                    pool.wait_ge(act_done, fp + p + 1)
                    pool.wait_ge(conv_up, (l * PAIRS + p + 1) * 4)
                    pool.wait_ge(hid_ready, fp + p)
                    pool.tensor_tensor(hidf, act_out, conv2[:, 1, :, :].rearrange("p c t -> p (c t)"), ALU.mult) \
                        .then_inc(scaled_done, 1)

            def mixer2(l):
                sum_squares(3 * DEPTH + 1 + 2 * l)
                zero(pool_u[:, :, 0:POOL_PAD], pads)
                zero(ghid.rearrange("p v m g n -> p (v m g) n")[:, :, NCMP:], pads)

                def cosines(n, k):
                    unit = TURNS[n][0]
                    pool.wait_ge(taken2, l * FILLS + unit)
                    if k >= 1:
                        pool.wait_ge(rot2_taken, l * len(TURNS) + TURN_OF_Q[k - 1] + 1)
                        pool.wait_ge(rope2_done, l * (len(TURNS) - 1) + ROPE_OF_Q[k - 1] + 1)
                    src = qa[:, 2 * k:2 * k + 2, :] if k < 2 else dqr[:, 2 * k - 4:2 * k - 2, :]
                    pool.tensor_tensor(ropec2, src, cos2, ALU.mult).then_inc(cos2_done, 1)

                for n, (unit, kind, k) in enumerate(TURNS):
                    if kind == "q":
                        cosines(n, k)
                pool.wait_ge(blk_split, (l + 1) * 2)
                zero(cpad[:, :, 0:CONV_PAD], pads)
                pool.wait_ge(taken2, l * FILLS + M2_AG)
                pool.wait_ge(pads, (l + 1) * 3)
                for n, (dst, src, g, w) in enumerate(((pool_a, pool_u, 0, 1), (pool_b, pool_a, 1, 2), (pool_a, pool_b, 2, 4),
                                                      (pool_b, pool_a, 3, 8))):
                    if n:
                        pool.wait_ge(pool_step, l * 4 + n)
                    a = 2 * w - 1
                    pool.tensor_tensor(dst[:, g:, a:], src[:, g:, a:], src[:, g:, a - w:PW - w], ALU.add).then_inc(pool_step, 1)
                for j in range(JOBS):
                    pool.wait_ge(rec2_done, rec_steps(l, j + 1))
                    for i in range(2):
                        for t, part in ((0, slice(0, P)), (1, slice(P, 3 * P))):
                            x = s2[:, j % 2, i, part]
                            rec = rec2[:, j % 2, t, i:i + 1].broadcast_to(x.shape)
                            pool.tensor_tensor(x, x, rec, ALU.mult).then_inc(p2_normed, 1)

            pool.wait_ge(c2_in_s, 16)
            with pool.Fori(0, DEPTH) as l:
                mixer2(l)
                ffn_conv(l)

        @block.vector
        def _(dve):
            def split_lo(slot, uses, n=UNIT):
                dve.wait_ge(hi_ready[slot], uses + 1)
                dve.tensor_tensor(wlo[:, slot, 0:n], raw[:, slot, 0:n], whi[:, slot, 0:n].bitcast(F32), ALU.subtract) \
                    .then_inc(lo_ready[slot], 1)

            def h_lo(hn, gain, c):
                dve.wait_ge(h_hi, KC * hn + c + 1)
                dve.scalar_tensor_tensor(hlo[:, c, :], xT[:, c, :], par_col(gain + c), hhi[:, c, :].bitcast(F32),
                                         ALU.mult, ALU.subtract).then_inc(h_ready, 1)

            def norm_rstd(n):
                dve.wait_ge(std_done, n + 1)
                dve.reciprocal(rstd, std).then_inc(rstd_ready, 1)
                dve.wait_ge(rstd_ready, n + 1)

            def update(a, done_slot, done_uses, scale, c):
                if c < KC - 2:
                    dve.wait_ge(acc_done, a * (KC // 2 - 1) + c // 2 + 1)
                else:
                    dve.wait_ge(used[done_slot], done_uses + 1)
                dve.scalar_tensor_tensor(xT[:, c, :], bank(4 + c // 2, (c % 2) * SEQ, SEQ), scale, xT[:, c, :],
                                         ALU.mult, ALU.add).then_inc(x_updated, 1)

            def ffn(uses, f, n):
                fp = f * PAIRS
                split_lo(2, uses(0))
                norm_rstd(n)

                def gate(p, slot, u):
                    dve.wait_ge(used[slot], u + 1)
                    dve.wait_ge(act_done, fp + p)
                    dve.tensor_tensor(gate_sb, bank(0).rearrange("p (c t) -> p c t", c=2), rstd_over(2), ALU.mult) \
                        .then_inc(gate_taken, 1)

                def hidden(p, slot, u):
                    dve.wait_ge(used[slot], u + 1)
                    dve.wait_ge(scaled_done, fp + p + 1)
                    dve.wait_ge(hid_hi, fp + p)
                    dve.wait_ge(hid_ready, fp + p)
                    dve.tensor_tensor(hidf, bank(1), scaled, ALU.mult).then_inc(up_taken, 1)

                def hidden_lo(p, buf):
                    dve.wait_ge(hid_hi, fp + p + 1)
                    dve.tensor_tensor(hidlo[:, buf, :, :], hidf.rearrange("p (c t) -> p c t", c=2),
                                      hidhi[:, buf, :, :].bitcast(F32), ALU.subtract).then_inc(hid_ready, 1)

                gate(0, 0, uses(0))
                hidden(0, 1, uses(0))
                split_lo(0, uses(0) + 1)
                hidden_lo(0, 0)
                with dve.Fori(0, (PAIRS - 1) // 2) as it:
                    for j in range(2):
                        p = it * 2 + (j + 1)
                        split_lo(1, uses(0) + p)
                        gate(p, 2, uses(0) + p - 1)
                        split_lo(2, uses(0) + p)
                        hidden(p, 0, uses(0) + p)
                        split_lo(0, uses(0) + p + 1)
                        hidden_lo(p, (j + 1) % 2)
                split_lo(1, uses(0) + PAIRS)

            def update_and_norm(a, slot, u, scale, hn, gain):
                for c in range(KC + 1):
                    if c < KC:
                        update(a, slot, u, scale, c)
                    if c >= 1:
                        h_lo(hn, gain, c - 1)

            for c in range(KC):
                dve.wait_ge(x_turned, c // 2 * 2 + 2)
                dve.tensor_copy(xT[:, c, :], bank(4 + c // 2, (c % 2) * SEQ, SEQ)).then_inc(x_updated, 1)
            split_lo(0, 0)
            split_lo(1, 0)
            dve.wait_ge(par_ready, len(PAR_TILES))
            dve.wait_ge(c1_in_s, 16)
            dve.wait_ge(setup_done, N_SETUP)

            def mixer1(l):
                s0 = FFN_UNITS

                def next_split(i):
                    s = s0 + i + 2
                    n = D if i + 2 in (M1_OUT + 3, M1_OUT + 4) else UNIT
                    split_lo(s % RING, uses1(l, s), n)

                def done(i):
                    dve.wait_ge(used[(s0 + i) % RING], uses1(l, s0 + i) + 1)

                def take(i):
                    done(i)
                    out2 = bank(i % 2).rearrange("p (c t) -> p c t", c=2)
                    if i < M1_V or M1_SBQ <= i <= M1_SBK:
                        c = 2 * i if i < M1_V else 2 * (i - 3)
                        scale = QSCALE if i < M1_K or i == M1_SBQ else 1.0
                        dve.scalar_tensor_tensor(qk[:, c:c + 2, :], out2, scale, rstd_over(2), ALU.mult, ALU.mult) \
                            .then_inc(unit_taken, 1)
                    elif i < M1_GATE:
                        c = (i - M1_V) * UC if i < M1_SBQ else (M1_SBQ - M1_V) * UC
                        dve.tensor_tensor(vtok[:, :, c:c + UC], out2,
                                          rstd[:, SEQ:SEQ + TT].unsqueeze(2).broadcast_to([P, TT, UC]), ALU.mult) \
                            .then_inc(unit_taken, 1)
                    else:
                        c = 2 * (i - M1_GATE)
                        dve.tensor_tensor(gates[:, c:c + 2, :], out2, rstd_over(2), ALU.mult).then_inc(unit_taken, 1)

                def rope(i):
                    n = l * M1_V + i
                    two = lambda x: x.rearrange("p (c t) -> p c t", c=2)
                    dve.wait_ge(rot_done, n + 1)
                    dve.wait_ge(rope_done, n)
                    dve.tensor_tensor(two(m1["ropes"]), two(bank(3)), sin1, ALU.mult).then_inc(sin_done, 1)
                    dve.wait_ge(cos_done, n + 1)
                    dve.wait_ge(sin_done, n + 1)
                    dve.tensor_tensor(qk[:, 2 * i:2 * i + 2, :], two(m1["ropec"]), two(m1["ropes"]), ALU.add) \
                        .then_inc(rope_done, 1)

                def softmax(hs):
                    n = l * G1_HEADS + hs
                    b = hs % 2
                    dve.wait_ge(s_done, n + 1)
                    if hs >= 2:
                        dve.wait_ge(t_done, (n - 1) * NG)
                    parts = ((1, s1[:, b, 0:NG * SEQ], banks(2, NG * SEQ), mask1), (0, s1[:, b, NG * SEQ:], bank(4, 0, NG * P), mask0))
                    for t, s, src, mask in parts:
                        dve.scalar_tensor_tensor(s, src, -1.0, mask, ALU.mult, ALU.add).then_inc(s_taken, 1)
                    for t, s, src, mask in parts:
                        dve.wait_ge(s_taken, 2 * n + 2 - t)
                        dve.tensor_reduce(mn1[:, b, t:t + 1], s, AX.X, ALU.min).then_inc(min_done, 1)

                def denominators(hs):
                    n = l * G1_HEADS + hs
                    dve.wait_ge(p_done, 2 * n + 2)
                    dve.reciprocal(rec1[:, hs % 2, :], den1[:, hs % 2, :]).then_inc(rec_done, 1)

                def masked(dst, src):
                    for a, m, w in ((0, past0, SEQ), (SBH * SEQ, past1, P)):
                        d, s = (x[:, a:a + SBH * w].rearrange("p (h t) -> p h t", h=SBH) for x in (dst, src))
                        dve.tensor_tensor(d, s, m, ALU.mult).then_inc(sb_step, 1)

                for i in range(M1_PROJ):
                    next_split(i)
                    if i == 0:
                        norm_rstd(3 * l + 1)
                    if i - 1 in SCORES_AT:
                        softmax(SCORES_AT.index(i - 1))
                    if i == SB_AT + 1:
                        dve.wait_ge(ob_hi, 2 * l + 1)
                        dve.tensor_tensor(brlo[:, 0, 0:2, :], bank(7).rearrange("p (c t) -> p c t", c=2),
                                          brhi[:, 0, 0:2, :].bitcast(F32), ALU.subtract).then_inc(ob_ready, 1)
                        dve.wait_ge(sb_ln, l + 1)
                        dve.scalar_tensor_tensor(sb_b, banks(2, SBN), 0.0, sb_a, ALU.max, ALU.add).then_inc(sb_step, 1)
                        dve.wait_ge(sb_step, l * SB_STEPS + 1)
                        masked(sb_a, sb_b)
                        dve.wait_ge(sb_step, l * SB_STEPS + 3)
                        dve.tensor_tensor(sb_b, banks(2, SBN), sb_b, ALU.subtract).then_inc(sb_step, 1)
                    if i == SB_AT + 3:
                        dve.wait_ge(sb_after, l + 1)
                        dve.tensor_tensor(sb_b, banks(2, SBN), sb_b, ALU.add).then_inc(sb_step, 1)
                    take(i)
                    if 1 <= i <= M1_V:
                        rope(i - 1)
                    if i - 1 in SCORES_AT:
                        denominators(SCORES_AT.index(i - 1))
                next_split(M1_PROJ)
                dve.wait_ge(ob_hi, 2 * l + 2)
                dve.tensor_tensor(brlo[:, 0, 2:4, :], bank(5).rearrange("p (c t) -> p c t", c=2),
                                  brhi[:, 0, 2:4, :].bitcast(F32), ALU.subtract).then_inc(ob_ready, 1)
                dve.wait_ge(gate_on, (l + 1) * (M1_PROJ - M1_GATE))
                tmp = m1["ropes"].rearrange("p (c t) -> p c t", c=2)

                def y_lo(c):
                    dve.wait_ge(y_hi, l * KC + c + 1)
                    dve.tensor_tensor(hlo[:, c, :], mixed1[:, c, :], hhi[:, c, :].bitcast(F32), ALU.subtract) \
                        .then_inc(y_ready, 1)

                for c in range(KC):
                    if c < KC - 1:
                        dve.wait_ge(wp_done, l * (KC - 1) + c + 1)
                    else:
                        done(M1_PROJ)
                        done(M1_PROJ + 1)
                    for br, dst in ((0, mixed1[:, c, :]), (1, tmp[:, c % 2, :])):
                        dve.tensor_tensor(dst, gates[:, br * KC + c, :], bank(c % 2, br * SEQ, SEQ), ALU.mult) \
                            .then_inc(gated, 1)
                    dve.wait_ge(gated, 2 * (l * KC + c + 1))
                    dve.tensor_tensor(mixed1[:, c, :], mixed1[:, c, :], tmp[:, c % 2, :], ALU.add).then_inc(y_done, 1)
                    if c >= 1:
                        y_lo(c - 1)
                y_lo(KC - 1)
                for i in range(M1_PROJ + 1, M1_END):
                    next_split(i)

            with dve.Fori(0, DEPTH) as l:
                for c in range(KC):
                    h_lo(3 * l, C_FFN1 + KC * l, c)
                ffn(lambda s: uses1(l, s), 2 * l, 3 * l)
                update_and_norm(3 * l, 2, uses1(l, 0) + PAIRS - 1, 0.5, 3 * l + 1, C_MIX + KC * l)
                mixer1(l)
                last = FFN_UNITS + M1_END - 1
                update_and_norm(3 * l + 1, last % RING, uses1(l, last), 1.0, 3 * l + 2, C_FFN2 + KC * l)
                ffn(lambda s: uses1(l, FFN_UNITS + M1_END + s), 2 * l + 1, 3 * l + 2)
                for c in range(KC):
                    update(3 * l + 2, 2, uses1(l, FFN_UNITS + M1_END) + PAIRS - 1, 0.5, c)
            norm_rstd(3 * DEPTH)
            for c in range(KC):
                dve.scalar_tensor_tensor(xT[:, c, :], xT[:, c, :], par_col(C_FINAL + c), rstd_b, ALU.mult, ALU.mult) \
                    .then_inc(x_updated, 1)

            def post_update(m, n, gain, split=None):
                dve.wait_ge(post_std, m + 1)
                dve.reciprocal(rstd_b, std[:, 0:SEQ]).then_inc(post_rstd, 1)
                dve.wait_ge(post_rstd, m + 1)

                def scaled_chunk(c):
                    dve.scalar_tensor_tensor(post_t[:, c, :], bank(4 + c // 2, (c % 2) * SEQ, SEQ), par_col(gain + c), rstd_b,
                                             ALU.mult, ALU.mult).then_inc(post_step, 1)

                scaled_chunk(0)
                for c in range(KC):
                    if c + 1 < KC:
                        scaled_chunk(c + 1)
                    dve.wait_ge(post_step, m * KC + c + 1)
                    dve.tensor_tensor(xT[:, c, :], xT[:, c, :], post_t[:, c, :], ALU.add).then_inc(x_updated, 1)
                    if split is not None and c >= 1:
                        h_lo(*split, c - 1)
                if split is not None:
                    h_lo(*split, KC - 1)

            def ffn_conv(uses, l):
                fp = (2 * DEPTH + l) * PAIRS
                cp = l * PAIRS
                split_lo(2, uses(0))
                norm_rstd(3 * DEPTH + 2 + 2 * l)
                dve.wait_ge(pad_zero, l + 1)

                def take(p, w, slot, u):
                    dve.wait_ge(used[slot], u + 1)
                    dve.wait_ge(conv_first, (cp + p) * 4)
                    dve.wait_ge((conv_gate, conv_up)[w], (cp + p) * 4)
                    dve.tensor_tensor(pad2[:, w, :, 2:], bank(w).rearrange("p (c t) -> p c t", c=2), rstd_over(2), ALU.mult) \
                        .then_inc((gate_taken, up_taken)[w], 1)

                def taps(p, w):
                    done = (conv_gate, conv_up)[w]
                    for tap in (1, 0):
                        for c in range(2):
                            ch = C_FCONV + l * (4 * FCH) + w * (FCH // 2) + p * 2 + c
                            if tap:
                                dve.wait_ge(conv_first, (cp + p) * 4 + 2 * w + c + 1)
                            else:
                                dve.wait_ge(done, (cp + p) * 4 + c + 1)
                            dve.scalar_tensor_tensor(conv2[:, w, c, :], pad2[:, w, c, tap:tap + SEQ], par_col(ch + tap * FCH),
                                                     conv2[:, w, c, :], ALU.mult, ALU.add).then_inc(done, 1)

                def hidden_lo(p, buf):
                    dve.wait_ge(hid_hi, fp + p + 1)
                    dve.tensor_tensor(hidlo[:, buf, :, :], hidf.rearrange("p (c t) -> p c t", c=2),
                                      hidhi[:, buf, :, :].bitcast(F32), ALU.subtract).then_inc(hid_ready, 1)

                take(0, 0, 0, uses(0))
                taps(0, 0)
                take(0, 1, 1, uses(0))
                taps(0, 1)
                split_lo(0, uses(0) + 1)
                hidden_lo(0, 0)
                with dve.Fori(0, (PAIRS - 1) // 2) as it:
                    for j in range(2):
                        p = it * 2 + (j + 1)
                        split_lo(1, uses(0) + p)
                        take(p, 0, 2, uses(0) + p - 1)
                        split_lo(2, uses(0) + p)
                        taps(p, 0)
                        take(p, 1, 0, uses(0) + p)
                        split_lo(0, uses(0) + p + 1)
                        taps(p, 1)
                        hidden_lo(p, (j + 1) % 2)
                split_lo(1, uses(0) + PAIRS)

            def mixer2(l):
                two = lambda x: x.rearrange("p (c t) -> p c t", c=2)
                rstd_t = rstd[:, SEQ:SEQ + TT]

                def next_split(i):
                    n = {M2_AG: KC * 24, M2_OUT + 3: D, M2_OUT + 4: D}.get(i + 2, UNIT)
                    split_lo((i + 2) % RING, uses2(l, i + 2), n)

                def done(i):
                    dve.wait_ge(used[i % RING], uses2(l, i) + 1)

                def take(i):
                    done(i)
                    f = fill_of(i)
                    src = two(bank(f % 2))
                    if i in K_UNITS:
                        k = K_UNITS[i]
                        dve.tensor_tensor(ktmp[:, k, :], bank(f % 2, 0, SEQ), rstd_b, ALU.mult)
                        dve.tensor_tensor(vt[:, k, :, :], bank(f % 2, SEQ, SEQ).rearrange("p (t n) -> p t n", t=TT),
                                          rstd_t.unsqueeze(2).broadcast_to([P, TT, P]), ALU.mult).then_inc(taken2, 1)
                        return
                    if i == M2_AG:
                        dve.tensor_tensor(ga, bank(f % 2, 0, TT * 24).rearrange("p (t n) -> p t n", t=TT),
                                          rstd_t.unsqueeze(2).broadcast_to([P, TT, 24]), ALU.mult).then_inc(taken2, 1)
                        return
                    scale = None
                    if i < M2_CMP:
                        dst, scale = qa[:, 2 * i:2 * i + 2, :], QSCALE
                    elif i == M2_CMP:
                        dst = cmp_kv
                    elif M2_DQ <= i < M2_DKV:
                        c = 2 * (i - M2_DQ)
                        dst, scale = dqr[:, c:c + 2, :], QSCALE
                    elif i < M2_CONV + 2:
                        c = 2 * (i - M2_CONV)
                        dst = conv_a[:, c:c + 2, :]
                    elif i < M2_POOL:
                        c = 2 * (i - M2_CONV - 2)
                        if i == M2_CONV + 2:
                            dve.wait_ge(pads, (l + 1) * 3)
                        dst = cpad[:, c:c + 2, CONV_PAD:]
                    elif i < M2_AG:
                        c = 2 * (i - M2_POOL)
                        dst = pool_u[:, c:c + 2, POOL_PAD:]
                    else:
                        k, j = divmod(i - M2_GATE, 6)
                        dst = gate_buf[:, k % 2, 2 * j:2 * j + 2, :]
                    if scale is None:
                        dve.tensor_tensor(dst, src, rstd_over(2), ALU.mult).then_inc(taken2, 1)
                    else:
                        dve.scalar_tensor_tensor(dst, src, scale, rstd_over(2), ALU.mult, ALU.mult).then_inc(taken2, 1)

                def turn(n, kind, k):
                    dve.wait_ge(rot2_done, l * len(TURNS) + n + 1)
                    if kind == "q":
                        r = l * (len(TURNS) - 1) + ROPE_OF_Q[k]
                        dve.wait_ge(rope2_done, r)
                        dve.tensor_tensor(ropes2, two(bank(4)), sin2, ALU.mult).then_inc(rot2_taken, 1)
                        dve.wait_ge(rot2_taken, l * len(TURNS) + n + 1)
                        dve.wait_ge(cos2_done, l * 4 + k + 1)
                        dst = qr[:, 2 * k:2 * k + 2, :] if k < 2 else dqr[:, 2 * k - 4:2 * k - 2, :]
                        dve.tensor_tensor(dst, ropec2, ropes2, ALU.add).then_inc(rope2_done, 1)
                    elif kind == "k":
                        r = l * (len(TURNS) - 1) + ROPE_OF_K[k]
                        dve.wait_ge(rope2_done, r)
                        dve.tensor_tensor(kd[:, k, :, :], two(bank(3)), cos2, ALU.mult).then_inc(rot2_step, 1)
                        dve.tensor_tensor(ropes2, two(bank(4)), sin2, ALU.mult).then_inc(rot2_taken, 1)
                        dve.wait_ge(rot2_taken, l * len(TURNS) + n + 1)
                        dve.tensor_tensor(kd[:, k, :, :], kd[:, k, :, :], ropes2, ALU.add).then_inc(rope2_done, 1)
                    else:
                        for v in range(2):
                            pos = par[:, bass.ds(C_POS + (l * 2 + v) * CJ, CJ)]
                            for half in range(2):
                                lane = slice(half * DH, half * DH + DH)
                                tok = bank(3 + v)[lane, :].rearrange("p (g n j h) -> p h j g n", g=KVH, j=CJ // 2, h=2)
                                for jj in range(2):
                                    js = slice(jj * CJ // 2, (jj + 1) * CJ // 2)
                                    dve.tensor_tensor(blkf[lane, v, js, :, :], tok[:, half, :, :, jj:jj + NCMP],
                                                      pos[lane, js].unsqueeze(2).unsqueeze(3).broadcast_to([DH, CJ // 2, KVH, NCMP]),
                                                      ALU.add).then_inc(blk_ready, 1)
                        dve.wait_ge(blk_ready, (l + 1) * 8)
                        dve.tensor_copy(fix16, par[:, 0:POOL_PAD]).then_inc(rot2_taken, 1)

                def blk_low():
                    for v in range(2):
                        dve.wait_ge(blk_hi_done, l * 2 + v + 1)
                        dve.tensor_tensor(blk_lo[:, v, :], blkf[:, v, :, :, :].rearrange("p j g n -> p (j g n)"),
                                          blk_hi[:, v, :].bitcast(F32), ALU.subtract).then_inc(blk_split, 1)

                def softmax(j):
                    n = l * JOBS + j
                    b = j % 2
                    dve.wait_ge(s2_done, n + 1)
                    if j >= 2:
                        dve.wait_ge(t2_done, n - 1)
                    dve.scalar_tensor_tensor(s2[:, b, :, :], ps[:, 2:4, 0:3 * P], -1.0, window if j < SWA_JOBS else causal,
                                             ALU.mult, ALU.add).then_inc(s2_taken, 1)
                    dve.wait_ge(s2_taken, n + 1)
                    m = mn_steps(l, j)
                    dve.tensor_reduce(mn2[:, b, 0, :], s2[:, b, :, 0:P], AX.X, ALU.min).then_inc(mn2_step, 1)
                    dve.tensor_reduce(mn2[:, b, 1, :], s2[:, b, :, P:], AX.X, ALU.min).then_inc(mn2_step, 1)
                    if j < SWA_JOBS:
                        sinks = neg_sinks[:, 2 * j:2 * j + 2].unsqueeze(1).broadcast_to([P, TT, 2])
                        dve.wait_ge(mn2_step, m + 2)
                        dve.tensor_tensor(mn2[:, b, :, :], mn2[:, b, :, :], sinks, ALU.min).then_inc(mn2_step, 1)
                        dve.wait_ge(mn2_step, m + 3)
                        dve.tensor_tensor(dsk[:, b, :, :], mn2[:, b, :, :], sinks, ALU.subtract).then_inc(mn2_step, 1)

                def denominators(j):
                    n = l * JOBS + j
                    b = j % 2
                    r = rec_steps(l, j)
                    if j < SWA_JOBS:
                        dve.wait_ge(p2_done, p_steps(l, j + 1))
                        dve.tensor_tensor(den2[:, b, :, :], den2[:, b, :, :], es[:, b, :, :], ALU.add).then_inc(rec2_done, 1)
                        dve.wait_ge(rec2_done, r + 1)
                        dve.reciprocal(rec2[:, b, :, :], den2[:, b, :, :]).then_inc(rec2_done, 1)
                    else:
                        h = j - SWA_JOBS
                        dve.wait_ge(p2_done, p_steps(l, j + 1))
                        dve.reciprocal(rec2[:, b, :, :], den2[:, b, :, :]).then_inc(rec2_done, 1)
                        dve.wait_ge(rec2_done, r + 1)
                        gate = ga.rearrange("p t (b h) -> p t b h", b=3)[:, :, 1:3, h]
                        dve.tensor_tensor(rec2[:, b, :, :], rec2[:, b, :, :], gate, ALU.mult).then_inc(rec2_done, 1)

                def compressed_softmax():
                    flat = sc.rearrange("p t h n -> p (t h) n")
                    dve.wait_ge(sc_half, (l + 1) * 2)
                    base = l * SC_STEPS
                    for t in range(TT):
                        dve.scalar_tensor_tensor(sc[:, t, :, :], bank(4, SEQ + t * P, P).rearrange("p (h n) -> p h n", n=CP), -1.0,
                                                 cmpadd[:, t, :].unsqueeze(1).broadcast_to([P, NSA_H, CP]), ALU.mult, ALU.add) \
                            .then_inc(sc_step, 1)
                    dve.wait_ge(sc_step, base + 2)
                    dve.tensor_reduce(mnc, flat, AX.X, ALU.min).then_inc(sc_step, 1)
                    dve.wait_ge(sc_step, base + 3)
                    dve.tensor_tensor(flat, flat, mnc.unsqueeze(2).broadcast_to([P, TT * NSA_H, CP]), ALU.subtract) \
                        .then_inc(sc_step, 1)

                def compressed_norm():
                    flat = sc.rearrange("p t h n -> p (t h) n")
                    base = l * SC_DEN
                    dve.wait_ge(sc_exp, l + 1)
                    dve.wait_ge(ga_on, l + 1)
                    dve.tensor_reduce(denc, flat, AX.X, ALU.add).then_inc(sc_den, 1)
                    dve.wait_ge(sc_den, base + 1)
                    dve.reciprocal(recc, denc).then_inc(sc_den, 1)
                    dve.wait_ge(sc_den, base + 2)
                    rec = recc.rearrange("p (t r g) -> p t r g", t=TT, r=GRP)
                    for t in range(TT):
                        dve.tensor_tensor(rec[:, t, :, :], rec[:, t, :, :], ga[:, t, 0:NSA_H].rearrange("p (g r) -> p r g", r=GRP),
                                          ALU.mult).then_inc(sc_den, 1)
                    dve.wait_ge(sc_den, base + 4)
                    dve.tensor_tensor(flat, flat, recc.unsqueeze(2).broadcast_to([P, TT * NSA_H, CP]), ALU.mult).then_inc(sc_den, 1)
                    dve.wait_ge(sc_den, base + 5)
                    for t in range(TT):
                        dve.tensor_tensor(sc[:, t, :, :], sc[:, t, :, :], cmp01[:, t, :].unsqueeze(1).broadcast_to([P, NSA_H, CP]),
                                          ALU.mult).then_inc(sc_den, 1)

                def pool_means():
                    dve.wait_ge(pool_step, (l + 1) * 4)
                    for g, w in enumerate(POOL_WINDOWS):
                        src = (pool_a, pool_b)[g % 2][:, g, :]
                        n = l * 12 + 3 * g
                        u = pool_u[:, g, :]
                        if g:
                            dve.wait_ge(pooled, n)
                        dve.tensor_tensor(fix16, src[:, POOL_PAD:2 * POOL_PAD], inv_count[:, g, :], ALU.mult).then_inc(pooled, 1)
                        dve.scalar_tensor_tensor(u[:, 2 * POOL_PAD:], src[:, 2 * POOL_PAD:], 1.0 / w, u[:, 2 * POOL_PAD:], ALU.mult,
                                                 ALU.subtract).then_inc(pooled, 1)
                        dve.wait_ge(pooled, n + 1)
                        dve.tensor_tensor(u[:, POOL_PAD:2 * POOL_PAD], fix16, u[:, POOL_PAD:2 * POOL_PAD], ALU.subtract) \
                            .then_inc(pooled, 1)

                def conv_taps(a, b):
                    for n in range(a, b):
                        tap, c = divmod(n, BRC)
                        w = par_col(C_CONVW + l * (CONVW * BRC) + tap * BRC + c)
                        x = cpad[:, c, tap:tap + SEQ]
                        if tap == 0:
                            dve.tensor_scalar(conv_acc[:, c, :], x, w, par_col(C_CONVB + BRC * l + c), ALU.mult, ALU.add) \
                                .then_inc(conv_step, 1)
                        else:
                            dve.wait_ge(conv_step, l * CONVW * BRC + n - BRC + 1)
                            dve.scalar_tensor_tensor(conv_acc[:, c, :], x, w, conv_acc[:, c, :], ALU.mult, ALU.add) \
                                .then_inc(conv_step, 1)

                def branch(k):
                    ia, ib = branch_units(k)
                    dve.wait_ge(gates_on, l * NBR + k + 1)

                    def y_lo(c):
                        dve.wait_ge(y2_hi, l * (KC // 2) + c + 1)
                        dve.tensor_tensor(hlo[:, 2 * c:2 * c + 2, :], mixed2[:, 2 * c:2 * c + 2, :],
                                          hhi[:, 2 * c:2 * c + 2, :].bitcast(F32), ALU.subtract).then_inc(y2_ready, 2)

                    for dp in range(KC // 2):
                        if dp < KC // 2 - 1:
                            dve.wait_ge(br_done, (l * NBR + k) * (KC // 2 - 1) + dp + 1)
                        else:
                            done(ia)
                            done(ib)
                        c = slice(2 * dp, 2 * dp + 2)
                        dst = mixed2[:, c, :] if k == 0 else gated_tmp
                        f = fill_of(ia, dp)
                        if k in range(1, NBR - 1) or k == NBR - 1 and dp == 0:
                            dve.wait_ge(gated2, (l * (NBR - 2) + k - 1) * (KC // 2) + dp)
                        elif k == NBR - 1:
                            dve.wait_ge(y2_done, l * (KC // 2) + dp)
                        dve.tensor_tensor(dst, gate_buf[:, k % 2, c, :], two(bank(f % 2)), ALU.mult).then_inc(taken2, 1)
                        if k:
                            dve.wait_ge(taken2, l * FILLS + f + 1)
                            dve.tensor_tensor(mixed2[:, c, :], mixed2[:, c, :], gated_tmp, ALU.add) \
                                .then_inc(gated2 if k < NBR - 1 else y2_done, 1)
                            if k == NBR - 1 and dp >= 1:
                                y_lo(dp - 1)
                    if k == NBR - 1:
                        y_lo(KC // 2 - 1)

                taps = CONVW * BRC
                conv_cut = [min(taps, -(-taps * n // CONV_STEPS)) for n in range(CONV_STEPS + 1)]
                for i in range(M2_OUT):
                    joint = i in second_of
                    if not joint:
                        next_split(i)
                    if i == 0:
                        norm_rstd(3 * DEPTH + 1 + 2 * l)
                    if i == M2_GATE - 3:
                        pool_means()
                    if i == 5:
                        blk_low()
                    if i == M2_CONV:
                        dve.wait_ge(small_in, (l + 1) * 16 * N_SMALL)
                        dve.tensor_scalar(neg_sinks, neg_sinks, -1.0, None, ALU.mult).then_inc(rot2_step, 1)
                    if i - 1 in job_scored:
                        softmax(job_scored[i - 1])
                    if i - 1 in job_turned and job_turned[i - 1] in OUTPUTS:
                        j = job_turned[i - 1]
                        buf, c = OUTPUTS[j]
                        dve.wait_ge(ob2_hi, l * N_OUT + sorted(OUTPUTS).index(j) + 1)
                        dve.tensor_tensor(brlo[:, buf, c:c + 2, :], two(bank(7)), brhi[:, buf, c:c + 2, :].bitcast(F32), ALU.subtract) \
                            .then_inc(ob2_ready, 1)
                    if i == CMP_AT + 1:
                        dve.wait_ge(kcvb_done, l + 1)
                        dve.tensor_copy(kc_t.rearrange("p g n -> p (g n)"), bank(4, 0, KVH * CP)).then_inc(kcvb_taken, 1)
                        dve.tensor_tensor(vb, bank(4, P, P), blockdiag, ALU.mult).then_inc(kcvb_taken, 1)
                    if i == CMP_AT + 2:
                        compressed_softmax()
                    if i == CMP_AT + 3:
                        compressed_norm()
                    if i == POOL_AT + 1:
                        for g in range(4):
                            dve.wait_ge(pool_hi, l * 4 + 4)
                            dve.scalar_tensor_tensor(brlo[:, 0, g, :], bank(5 + g // 2, (g % 2) * SEQ, SEQ),
                                                     par_col(C_POOLS + BRC * l + g), brhi[:, 0, g, :].bitcast(F32), ALU.mult,
                                                     ALU.subtract).then_inc(pool_lo, 1)
                    if i == CONV_FROM:
                        dve.wait_ge(cg_on, l + 1)
                        dve.tensor_tensor(cpad[:, :, CONV_PAD:], cpad[:, :, CONV_PAD:], conv_a, ALU.mult).then_inc(c_ready, 1)
                        dve.wait_ge(c_ready, l + 1)
                    if i == LN_AT + 1:
                        dve.wait_ge(ln_mean, l + 1)
                        dve.scalar_tensor_tensor(conv_acc, bank(4, 0, SEQ).unsqueeze(1).broadcast_to([P, BRC, SEQ]), -2.0, conv_acc,
                                                 ALU.mult, ALU.add).then_inc(ln_cent, 1)
                    if i == LN_AT + 2:
                        dve.wait_ge(ln_stdd, l + 1)
                        dve.reciprocal(ln_rstd, ln_std).then_inc(ln_step, 1)
                        dve.wait_ge(ln_step, l * 3 + 1)
                        dve.tensor_tensor(conv_acc, conv_acc, ln_rstd.unsqueeze(1).broadcast_to([P, BRC, SEQ]), ALU.mult) \
                            .then_inc(ln_step, 1)
                    if i == LN_AT + 3:
                        dve.wait_ge(silu_done, (l + 1) * 5)
                        dve.tensor_tensor(brlo[:, 0, :, :], silu_out, brhi[:, 0, :, :].bitcast(F32), ALU.subtract) \
                            .then_inc(ln_step, 1)
                    if joint:
                        branch(second_of[i])
                        next_split(i)
                    elif i not in first_of and not M2_W1 <= i < M2_GATE:
                        take(i)
                    for n, (unit, kind, k) in enumerate(TURNS):
                        if unit == i:
                            turn(n, kind, k)
                    if i - 1 in job_scored:
                        denominators(job_scored[i - 1])
                    if CONV_FROM <= i < CONV_FROM + CONV_STEPS:
                        conv_taps(conv_cut[i - CONV_FROM], conv_cut[i - CONV_FROM + 1])
                for i in range(M2_OUT, M2_END):
                    next_split(i)

            dve.wait_ge(c2_in_s, 16)
            with dve.Fori(0, DEPTH) as l:
                for c in range(KC):
                    h_lo(3 * DEPTH + 2 * l, C_MIXPRE + KC * l, c)
                mixer2(l)
                post_update(2 * l, 3 * DEPTH + 1 + 2 * l, C_MIXPOST + KC * l, (3 * DEPTH + 1 + 2 * l, C_FFNPRE + KC * l))
                ffn_conv(lambda s: uses2(l, M2_END + s), l)
                post_update(2 * l + 1, 3 * DEPTH + 2 + 2 * l, C_FFNPOST + KC * l)
            for t in range(TT):
                for n in range(2):
                    dve.wait_ge(out_turned, 2 * t + n + 1)
                    dve.tensor_copy(otok[:, t, n * 512:(n + 1) * 512], bank(2 * t + n)).then_inc(out_copied, 1)


_NAMES = [
    "x", "norm_ffn1", "ffn1_w_gate", "ffn1_w_up", "ffn1_w_down", "norm_mix", "w_in", "w_proj_dil", "w_proj_sb",
    "w_out", "norm_ffn2", "ffn2_w_gate", "ffn2_w_up", "ffn2_w_down", "norm_final", "norm_mix_pre_2",
    "norm_mix_post_2", "norm_ffn_pre_2", "norm_ffn_post_2", "w_in_2", "nsa_cmp_pos_2", "nsa_cmp_w1_2",
    "nsa_cmp_w2_2", "swa_sinks_2", "conv_w_2", "conv_b_2", "conv_ln_g_2", "conv_ln_b_2", "pool_w_2",
    "pool_scale_2", "w_branch_2", "w_gate_2", "w_o_2", "ffn_w_up_2", "ffn_conv_w_2", "ffn_conv_b_2",
    "ffn_w_down_2"]


def kernel(**inputs):
    import concourse.bacc as bacc
    from concourse.bass_utils import run_bass_kernel_spmd

    nc = bacc.Bacc("TRN2", target_bir_lowering=False, num_devices=1)
    arrays = {f"in_{n}": np.ascontiguousarray(inputs[n]) for n in _NAMES}
    for n, table in zip(("ident", "tables1", "tables2"), shape_consts()):
        arrays[f"const_{n}"] = table
    aps = {n: nc.dram_tensor(n, a.shape, mybir.dt.from_np(a.dtype), kind="ExternalInput").ap() for n, a in arrays.items()}
    out = nc.dram_tensor("out", (1, SEQ, D), F32, kind="ExternalOutput").ap()
    hybrid_network(nc, {n: aps[f"in_{n}"] for n in _NAMES}, aps["const_ident"], aps["const_tables1"],
                   aps["const_tables2"], out)
    r = run_bass_kernel_spmd(nc, [arrays], core_ids=[0])
    return r.results[0]["out"]
```
